# Optimizing a Trainium2 kernel written in Bass

```python
import math
import jax
import jax.numpy as jnp
from jax import lax
import numpy as np
import jax, jax.numpy as jnp

D_MODEL = 1024
BATCH = 1
SEQ = 256
DEPTH = 1

N_HEADS = 8
HEAD_DIM = 64
ATTN_WIDTH = N_HEADS * HEAD_DIM
MOBA_BLOCK = 256
MOBA_TOPK = 3
MOBA_Q_CHUNK = 64
POOL_WINDOWS = (2, 4, 8, 16)
POOL_GROUPS = len(POOL_WINDOWS)
POOL_WIDTH = D_MODEL // 2
POOL_GROUP_WIDTH = POOL_WIDTH // POOL_GROUPS
N_BRANCHES = 2
IN_WIDTH = 3 * ATTN_WIDTH + POOL_WIDTH + N_BRANCHES * D_MODEL
REL_BUCKETS = 32
REL_MAX_DIST = 128
N_EXPERT_GROUPS = 4
EXPERTS_PER_GROUP = 8
N_EXPERTS = N_EXPERT_GROUPS * EXPERTS_PER_GROUP
EXPERT_TOPK = 2
D_EXPERT = D_MODEL // 2
N_MOD = 6
EPS = 1e-6
NEG_INF = -1e30


def rms_norm(x, g):
    xf = x.astype(jnp.float32)
    xf = xf * lax.rsqrt(jnp.mean(xf * xf, axis=-1, keepdims=True) + EPS)
    return (xf * g.astype(jnp.float32)).astype(x.dtype)

def t5_bucket(rel):
    n = jnp.maximum(rel, 0)
    max_exact = REL_BUCKETS // 2
    nf = jnp.maximum(n, 1).astype(jnp.float32)
    large = max_exact + (jnp.log(nf / max_exact) / math.log(REL_MAX_DIST / max_exact)
                         * (REL_BUCKETS - max_exact)).astype(jnp.int32)
    large = jnp.minimum(large, REL_BUCKETS - 1)
    return jnp.where(n < max_exact, n, large)

def moba_attention(q, k, v, rel_bias):
    B, S, H, Dh = q.shape
    nb = -(-S // MOBA_BLOCK)
    pad = nb * MOBA_BLOCK - S
    topk = min(MOBA_TOPK, nb)
    scale = Dh ** -0.5
    qh = q.transpose(0, 2, 1, 3)
    kp = jnp.pad(k.transpose(0, 2, 1, 3), ((0, 0), (0, 0), (0, pad), (0, 0)))
    vp = jnp.pad(v.transpose(0, 2, 1, 3), ((0, 0), (0, 0), (0, pad), (0, 0)))
    kb = kp.reshape(B, H, nb, MOBA_BLOCK, Dh)
    vb = vp.reshape(B, H, nb, MOBA_BLOCK, Dh)
    k_mean = jnp.mean(kb.astype(jnp.float32), axis=3)
    bias_t = rel_bias.T
    b_idx = jnp.arange(B)[:, None, None, None]
    h_idx = jnp.arange(H)[None, :, None, None]
    h_idx5 = jnp.arange(H)[None, :, None, None, None]
    blk_offsets = jnp.arange(MOBA_BLOCK)

    def attend_chunk(ci):
        q0 = ci * MOBA_Q_CHUNK
        blk = q0 // MOBA_BLOCK
        qc = lax.dynamic_slice_in_dim(qh, q0, MOBA_Q_CHUNK, axis=2)
        qpos = q0 + jnp.arange(MOBA_Q_CHUNK)
        gate = jnp.einsum('bhqd,bhnd->bhqn', qc.astype(jnp.float32), k_mean)
        gate = jnp.where(jnp.arange(nb) < blk, gate, -jnp.inf)
        _, sel = lax.top_k(gate, topk)
        sel_valid = sel < blk
        ks = kb[b_idx, h_idx, sel]
        vs = vb[b_idx, h_idx, sel]
        s_sel = jnp.einsum('bhqd,bhqjkd->bhqjk', qc, ks).astype(jnp.float32) * scale
        kpos_sel = sel[..., None] * MOBA_BLOCK + blk_offsets
        bucket_sel = t5_bucket(qpos[None, None, :, None, None] - kpos_sel)
        s_sel = s_sel + bias_t[h_idx5, bucket_sel].astype(jnp.float32)
        s_sel = jnp.where(sel_valid[..., None], s_sel, NEG_INF)
        ko = lax.dynamic_index_in_dim(kb, blk, axis=2, keepdims=False)
        vo = lax.dynamic_index_in_dim(vb, blk, axis=2, keepdims=False)
        s_own = jnp.einsum('bhqd,bhkd->bhqk', qc, ko).astype(jnp.float32) * scale
        rel_own = qpos[:, None] - (blk * MOBA_BLOCK + blk_offsets)[None, :]
        s_own = s_own + bias_t[:, t5_bucket(rel_own)][None].astype(jnp.float32)
        s_own = jnp.where(rel_own >= 0, s_own, NEG_INF)
        logits = jnp.concatenate(
            [s_sel.reshape(B, H, MOBA_Q_CHUNK, topk * MOBA_BLOCK), s_own], axis=-1)
        p = jax.nn.softmax(logits, axis=-1).astype(v.dtype)
        p_sel = p[..., :topk * MOBA_BLOCK].reshape(B, H, MOBA_Q_CHUNK, topk, MOBA_BLOCK)
        p_own = p[..., topk * MOBA_BLOCK:]
        return (jnp.einsum('bhqjk,bhqjkd->bhqd', p_sel, vs)
                + jnp.einsum('bhqk,bhkd->bhqd', p_own, vo))

    out = lax.map(attend_chunk, jnp.arange(S // MOBA_Q_CHUNK))
    return out.transpose(1, 0, 3, 2, 4).reshape(B, S, H * Dh)

def pool_mixer(u, pool_w, pool_scale):
    B, S, P = u.shape
    uf = u.astype(jnp.float32)
    cs = jnp.pad(jnp.cumsum(uf, axis=1), ((0, 0), (1, 0), (0, 0)))
    t = jnp.arange(S)
    outs = []
    for g, w in enumerate(POOL_WINDOWS):
        lo_c, hi_c = g * POOL_GROUP_WIDTH, (g + 1) * POOL_GROUP_WIDTH
        csg = cs[..., lo_c:hi_c]
        lo = jnp.maximum(t + 1 - w, 0)
        cnt = (t + 1 - lo).astype(jnp.float32)
        mean = (csg[:, 1:] - csg[:, lo]) / cnt[None, :, None]
        d = (mean - uf[..., lo_c:hi_c]).astype(u.dtype)
        outs.append(jnp.einsum('bsc,cd->bsd', d, pool_w[g]))
    return jnp.concatenate(outs, axis=-1) * pool_scale

def hier_moe(h, w_rg, b_rg, w_re, b_re, w_g, w_u, w_d):
    B, S, D = h.shape
    N = B * S
    hf = h.reshape(N, D)
    z_group = (hf @ w_rg).astype(jnp.float32) + b_rg.astype(jnp.float32)
    p_group = jax.nn.softmax(z_group, axis=-1)
    pg_top, g_idx = lax.top_k(p_group, 1)
    z_exp = ((hf @ w_re).astype(jnp.float32) + b_re.astype(jnp.float32)).reshape(
        N, N_EXPERT_GROUPS, EXPERTS_PER_GROUP)
    z_in_group = z_exp[jnp.arange(N), g_idx[:, 0]]
    ze_top, e_idx = lax.top_k(z_in_group, EXPERT_TOPK)
    weights = pg_top * jax.nn.softmax(ze_top, axis=-1)
    expert_id = g_idx * EXPERTS_PER_GROUP + e_idx
    combine = jnp.einsum('nk,nke->ne', weights,
                         jax.nn.one_hot(expert_id, N_EXPERTS, dtype=jnp.float32)).astype(h.dtype)
    y = jnp.zeros_like(hf)
    for e in range(N_EXPERTS):
        act = jax.nn.silu(hf @ w_g[e]) * (hf @ w_u[e])
        y = y + combine[:, e:e + 1] * (act @ w_d[e])
    return y.reshape(B, S, D)

def first_inputs(seed: int = 0) -> dict:
    key = jax.random.key(seed)
    ks = jax.random.split(key, 22)
    f32 = jnp.float32
    D = D_MODEL
    PGW = POOL_GROUP_WIDTH

    def nrm(k, shape, s):
        return jax.random.normal(k, shape, f32) * s

    return {
        "x": nrm(ks[0], (BATCH, SEQ, D), 1.0),
        "c": nrm(ks[1], (BATCH, D), 1.0),
        "w_ada": nrm(ks[2], (DEPTH, D, N_MOD * D), 0.5 * D ** -0.5),
        "b_ada": nrm(ks[3], (DEPTH, N_MOD * D), 0.02),
        "norm1_g": 1.0 + nrm(ks[4], (DEPTH, D), 0.05),
        "w_in": nrm(ks[5], (DEPTH, D, IN_WIDTH), D ** -0.5),
        "b_gate": nrm(ks[6], (DEPTH, N_BRANCHES * D), 0.02),
        "rel_bias": nrm(ks[7], (REL_BUCKETS, N_HEADS), 0.5),
        "pool_w": nrm(ks[8], (DEPTH, POOL_GROUPS, PGW, PGW), PGW ** -0.5),
        "pool_scale": 1.0 + nrm(ks[9], (DEPTH, POOL_WIDTH), 0.1),
        "w_branch_attn": nrm(ks[10], (DEPTH, ATTN_WIDTH, D), ATTN_WIDTH ** -0.5),
        "w_branch_pool": nrm(ks[11], (DEPTH, POOL_WIDTH, D), POOL_WIDTH ** -0.5),
        "w_out": nrm(ks[12], (DEPTH, D, D), D ** -0.5),
        "norm2_g": 1.0 + nrm(ks[13], (DEPTH, D), 0.05),
        "w_router_group": nrm(ks[14], (DEPTH, D, N_EXPERT_GROUPS), D ** -0.5),
        "b_router_group": nrm(ks[15], (DEPTH, N_EXPERT_GROUPS), 0.01),
        "w_router_expert": nrm(ks[16], (DEPTH, D, N_EXPERTS), D ** -0.5),
        "b_router_expert": nrm(ks[17], (DEPTH, N_EXPERTS), 0.01),
        "w_expert_gate": nrm(ks[18], (DEPTH, N_EXPERTS, D, D_EXPERT), D ** -0.5),
        "w_expert_up": nrm(ks[19], (DEPTH, N_EXPERTS, D, D_EXPERT), D ** -0.5),
        "w_expert_down": nrm(ks[20], (DEPTH, N_EXPERTS, D_EXPERT, D), D_EXPERT ** -0.5),
        "norm_f_g": 1.0 + nrm(ks[21], (D,), 0.05),
    }

def first_block(x, c, w_ada, b_ada, norm1_g, w_in, b_gate, rel_bias, pool_w, pool_scale,
              w_branch_attn, w_branch_pool, w_out, norm2_g, w_router_group, b_router_group,
              w_router_expert, b_router_expert, w_expert_gate, w_expert_up, w_expert_down,
              norm_f_g):
    B, S, D = x.shape
    c_act = jax.nn.silu(c)
    split_pts = [ATTN_WIDTH, 2 * ATTN_WIDTH, 3 * ATTN_WIDTH, 3 * ATTN_WIDTH + POOL_WIDTH]
    for l in range(DEPTH):
        mod = (c_act @ w_ada[l] + b_ada[l])[:, None, :]
        shift1, scale1, gate1, shift2, scale2, gate2 = jnp.split(mod, N_MOD, axis=-1)
        h = rms_norm(x, norm1_g[l]) * (1 + scale1) + shift1
        proj = h @ w_in[l]
        q, k, v, u, z_gate = jnp.split(proj, split_pts, axis=-1)
        q = q.reshape(B, S, N_HEADS, HEAD_DIM)
        k = k.reshape(B, S, N_HEADS, HEAD_DIM)
        v = v.reshape(B, S, N_HEADS, HEAD_DIM)
        y_attn = moba_attention(q, k, v, rel_bias) @ w_branch_attn[l]
        y_pool = pool_mixer(u, pool_w[l], pool_scale[l]) @ w_branch_pool[l]
        g_attn, g_pool = jnp.split(jax.nn.sigmoid(z_gate + b_gate[l]), N_BRANCHES, axis=-1)
        mixed = (g_attn * y_attn + g_pool * y_pool) @ w_out[l]
        x = x + gate1 * mixed
        h2 = rms_norm(x, norm2_g[l]) * (1 + scale2) + shift2
        y_moe = hier_moe(h2, w_router_group[l], b_router_group[l], w_router_expert[l],
                         b_router_expert[l], w_expert_gate[l], w_expert_up[l], w_expert_down[l])
        x = x + gate2 * y_moe
    return rms_norm(x, norm_f_g)


DEPTH_2 = 2

HGRN_WIDTH = D_MODEL // 4
HGRN_HEADS = HGRN_WIDTH // HEAD_DIM
HGRN_CHUNK = 64
FOURIER_WIDTH = D_MODEL // 4
FOURIER_GROUPS = FOURIER_WIDTH // HEAD_DIM
ATTN_WIDTH_2 = D_MODEL // 2
ATTN_HEADS = ATTN_WIDTH_2 // HEAD_DIM
MIX_WIDTH = HGRN_WIDTH + FOURIER_WIDTH + ATTN_WIDTH_2
DILATED_PATTERNS = ((128, 1), (512, 4), (2048, 16))
ROPE_THETA = 10000.0
D_FF = 4 * D_MODEL
RMS_EPS = 1e-6
NEG_BIG = -1e30
IN_SPLITS = (HGRN_WIDTH, HGRN_WIDTH, HGRN_WIDTH, HGRN_WIDTH, HGRN_WIDTH, FOURIER_WIDTH, ATTN_WIDTH_2, ATTN_WIDTH_2, ATTN_WIDTH_2)
IN_WIDTH_2 = sum(IN_SPLITS)
SPLIT_POINTS = [sum(IN_SPLITS[:i + 1]) for i in range(len(IN_SPLITS) - 1)]


def rms_norm_2(x, w):
    xf = x.astype(jnp.float32)
    y = xf * lax.rsqrt(jnp.mean(xf * xf, axis=-1, keepdims=True) + RMS_EPS)
    return (y * w.astype(jnp.float32)).astype(x.dtype)

def hgrn2_chunk_scan(q, k, v, log_f):
    B, H, S, dk = q.shape
    dv = v.shape[-1]
    C = HGRN_CHUNK
    n = S // C

    def chunked(t):
        return jnp.moveaxis(t.reshape(B, H, n, C, t.shape[-1]), 2, 0)

    tri = jnp.tril(jnp.ones((C, C), dtype=bool))[:, :, None]

    def step(state, inp):
        qc, kc, vc, gc = inp
        b = jnp.cumsum(gc, axis=-2)
        inter = jnp.einsum('bhtk,bhkv->bhtv', qc * jnp.exp(b), state)
        diff = b[..., :, None, :] - b[..., None, :, :]
        pair = jnp.where(tri, jnp.exp(jnp.where(tri, diff, 0.0)), 0.0)
        scores = jnp.einsum('bhtk,bhsk,bhtsk->bhts', qc, kc, pair)
        intra = jnp.einsum('bhts,bhsv->bhtv', scores, vc)
        b_last = b[..., -1:, :]
        new_state = (jnp.exp(b_last[..., 0, :])[..., None] * state
                     + jnp.einsum('bhsk,bhsv->bhkv', kc * jnp.exp(b_last - b), vc))
        return new_state, inter + intra

    init = jnp.zeros((B, H, dk, dv), dtype=jnp.float32)
    _, out = lax.scan(step, init, (chunked(q), chunked(k), chunked(v), chunked(log_f)))
    return jnp.moveaxis(out, 0, 2).reshape(B, H, S, dv)

def hgrn2_mixer(q_in, i_in, zf, zb, g_in, lb):
    B, S, W = q_in.shape
    H, dh = HGRN_HEADS, HEAD_DIM
    f32 = jnp.float32
    z = jnp.stack([zf, zb[:, ::-1]], axis=1).astype(f32)
    lbb = lb.astype(f32)[None, :, None, :]
    f = lbb + (1.0 - lbb) * jax.nn.sigmoid(z)
    log_f = jnp.log(f)
    k = 1.0 - f
    q = jax.nn.silu(q_in.astype(f32))
    v = i_in.astype(f32)
    q2 = jnp.stack([q, q[:, ::-1]], axis=1)
    v2 = jnp.stack([v, v[:, ::-1]], axis=1)

    def heads(t):
        return t.reshape(B, 2, S, H, dh).transpose(0, 1, 3, 2, 4).reshape(B, 2 * H, S, dh)

    o = hgrn2_chunk_scan(heads(q2), heads(k), heads(v2), heads(log_f)).reshape(B, 2, H, S, dh)
    o = o[:, 0] + o[:, 1][:, :, ::-1]
    o = o * lax.rsqrt(jnp.mean(o * o, axis=-1, keepdims=True) + RMS_EPS)
    o = o.transpose(0, 2, 1, 3).reshape(B, S, W)
    return o * jax.nn.silu(g_in.astype(f32))

def fourier_mixer(u):
    B, S, W = u.shape
    ug = u.astype(jnp.float32).reshape(B, S, FOURIER_GROUPS, W // FOURIER_GROUPS)
    y = jnp.fft.fft2(ug, axes=(1, 3), norm='ortho').real
    return y.reshape(B, S, W)

def rotary(t, positions):
    hd = t.shape[-1]
    inv_freq = ROPE_THETA ** (-jnp.arange(0, hd, 2, dtype=jnp.float32) / hd)
    ang = positions.astype(jnp.float32)[:, None, :, None] * inv_freq
    cos, sin = jnp.cos(ang), jnp.sin(ang)
    t1, t2 = t[..., :hd // 2], t[..., hd // 2:]
    return jnp.concatenate([t1 * cos - t2 * sin, t2 * cos + t1 * sin], axis=-1)

def dilated_window_attention(q, k, v, window, dilation):
    B, H, S, hd = q.shape
    d = dilation
    R = window // (2 * dilation)
    BLK = R
    L = S // d
    nb = -(-L // BLK)
    Lp = nb * BLK

    def sub(t):
        return t.reshape(B, H, L, d, hd).transpose(0, 1, 3, 2, 4)

    qs = jnp.pad(sub(q), ((0, 0), (0, 0), (0, 0), (0, Lp - L), (0, 0))).reshape(B, H, d, nb, BLK, hd)

    def key_blocks(t):
        tp = jnp.pad(sub(t), ((0, 0), (0, 0), (0, 0), (BLK, Lp - L + BLK), (0, 0))).reshape(B, H, d, nb + 2, BLK, hd)
        return jnp.concatenate([tp[:, :, :, :-2], tp[:, :, :, 1:-1], tp[:, :, :, 2:]], axis=-2)

    k3 = key_blocks(k)
    v3 = key_blocks(v)
    qj = jnp.arange(nb)[:, None, None] * BLK + jnp.arange(BLK)[None, :, None]
    kj = (jnp.arange(nb)[:, None, None] - 1) * BLK + jnp.arange(3 * BLK)[None, None, :]
    valid = (kj >= 0) & (kj < L) & (jnp.abs(qj - kj) <= R)
    s = jnp.einsum('bhrnqc,bhrnkc->bhrnqk', qs, k3)
    s = jnp.where(valid, s, NEG_BIG)
    lse = jax.nn.logsumexp(s, axis=-1)
    p = jnp.exp(s - lse[..., None])
    o = jnp.einsum('bhrnqk,bhrnkc->bhrnqc', p, v3)
    o = o.reshape(B, H, d, Lp, hd)[:, :, :, :L].transpose(0, 1, 3, 2, 4).reshape(B, H, S, hd)
    lse = lse.reshape(B, H, d, Lp)[..., :L].transpose(0, 1, 3, 2).reshape(B, H, S)
    return o, lse

def dilated_attention_mixer(cq, ck, cv, positions):
    B, S, W = cq.shape
    f32 = jnp.float32

    def heads(t):
        return t.astype(f32).reshape(B, S, ATTN_HEADS, HEAD_DIM).transpose(0, 2, 1, 3)

    q = rotary(heads(cq), positions) * (HEAD_DIM ** -0.5)
    k = rotary(heads(ck), positions)
    v = heads(cv)
    outs = []
    lses = []
    for window, dilation in DILATED_PATTERNS:
        o_p, lse_p = dilated_window_attention(q, k, v, window, dilation)
        outs.append(o_p)
        lses.append(lse_p)
    weights = jax.nn.softmax(jnp.stack(lses, axis=0), axis=0)
    o = jnp.sum(weights[..., None] * jnp.stack(outs, axis=0), axis=0)
    return o.transpose(0, 2, 1, 3).reshape(B, S, W)

def second_inputs(seed: int = 0) -> dict:
    key = jax.random.key(seed)
    ks = jax.random.split(key, 10)
    f32 = jnp.float32
    x = jax.random.normal(ks[0], (BATCH, SEQ, D_MODEL), f32)
    positions = jnp.broadcast_to(jnp.arange(SEQ, dtype=jnp.int32)[None, :], (BATCH, SEQ))
    attn_norm_w = 1.0 + 0.02 * jax.random.normal(ks[1], (DEPTH_2, D_MODEL), f32)
    w_in = jax.random.normal(ks[2], (DEPTH_2, D_MODEL, IN_WIDTH_2), f32) * D_MODEL ** -0.5
    hgrn_lower_bounds = 0.5 * jax.random.normal(ks[3], (DEPTH_2, 2, HGRN_WIDTH), f32)
    w_out = jax.random.normal(ks[4], (DEPTH_2, MIX_WIDTH, D_MODEL), f32) * MIX_WIDTH ** -0.5
    mlp_norm_w = 1.0 + 0.02 * jax.random.normal(ks[5], (DEPTH_2, D_MODEL), f32)
    w_up = jax.random.normal(ks[6], (DEPTH_2, D_MODEL, D_FF), f32) * D_MODEL ** -0.5
    w_down = jax.random.normal(ks[7], (DEPTH_2, D_FF, D_MODEL), f32) * D_FF ** -0.5
    final_norm_w = 1.0 + 0.02 * jax.random.normal(ks[8], (D_MODEL,), f32)
    return {"x": x, "positions": positions, "attn_norm_w": attn_norm_w, "w_in": w_in,
            "hgrn_lower_bounds": hgrn_lower_bounds, "w_out": w_out, "mlp_norm_w": mlp_norm_w,
            "w_up": w_up, "w_down": w_down, "final_norm_w": final_norm_w}

def second_block(x, positions, attn_norm_w, w_in, hgrn_lower_bounds, w_out, mlp_norm_w, w_up, w_down, final_norm_w):
    p_lb = jax.nn.softmax(hgrn_lower_bounds.astype(jnp.float32), axis=0)
    lb_all = jnp.cumsum(p_lb, axis=0) - p_lb[0:1]
    for layer in range(DEPTH_2):
        h = rms_norm_2(x, attn_norm_w[layer])
        proj = h @ w_in[layer]
        a_q, a_i, a_zf, a_zb, a_g, b_u, c_q, c_k, c_v = jnp.split(proj, SPLIT_POINTS, axis=-1)
        o_a = hgrn2_mixer(a_q, a_i, a_zf, a_zb, a_g, lb_all[layer]).astype(x.dtype)
        o_b = fourier_mixer(b_u).astype(x.dtype)
        o_c = dilated_attention_mixer(c_q, c_k, c_v, positions).astype(x.dtype)
        mixed = jnp.concatenate([o_a, o_b, o_c], axis=-1)
        x = x + mixed @ w_out[layer]
        h = rms_norm_2(x, mlp_norm_w[layer])
        x = x + jnp.square(jax.nn.relu(h @ w_up[layer])) @ w_down[layer]
    return rms_norm_2(x, final_norm_w)


def setup_inputs(seed=0):
    out = dict(first_inputs(seed))
    for name, value in second_inputs(seed + 1).items():
        if name != "x":
            out[name + "_2"] = value
    return out


def reference(
    x, c, w_ada, b_ada, norm1_g, w_in, b_gate, rel_bias, pool_w, pool_scale, w_branch_attn,
    w_branch_pool, w_out, norm2_g, w_router_group, b_router_group, w_router_expert,
    b_router_expert, w_expert_gate, w_expert_up, w_expert_down, norm_f_g, positions_2,
    attn_norm_w_2, w_in_2, hgrn_lower_bounds_2, w_out_2, mlp_norm_w_2, w_up_2, w_down_2,
    final_norm_w_2,
):
    x = first_block(
        x, c, w_ada, b_ada, norm1_g, w_in, b_gate, rel_bias, pool_w, pool_scale, w_branch_attn,
        w_branch_pool, w_out, norm2_g, w_router_group, b_router_group, w_router_expert,
        b_router_expert, w_expert_gate, w_expert_up, w_expert_down, norm_f_g,
    )
    return second_block(
        x, positions_2, attn_norm_w_2, w_in_2, hgrn_lower_bounds_2, w_out_2, mlp_norm_w_2,
        w_up_2, w_down_2, final_norm_w_2,
    )


_drawn_inputs = setup_inputs


def setup_inputs(seed=0):
    import zlib

    import numpy as np

    out = dict(_drawn_inputs(seed))
    spreads = {}
    factors = {'norm1_g': 3.507,
     'b_gate': 8.0,
     'rel_bias': 2.692,
     'b_router_group': 8.0,
     'b_router_expert': 6.841,
     'attn_norm_w_2': 3.903,
     'hgrn_lower_bounds_2': 4.699,
     'final_norm_w_2': 2.698}
    for name, (base, spread) in spreads.items():
        noise = np.random.default_rng([zlib.crc32(name.encode()), seed]).standard_normal(out[name].shape)
        drawn = base * np.exp(spread * noise) if base else spread * noise
        out[name] = jnp.asarray(drawn.astype(out[name].dtype))
    for name, factor in factors.items():
        out[name] = (out[name] * factor).astype(out[name].dtype)
    return out
```

```python
import concourse.bass as bass
import concourse.mybir as mybir
import numpy as np
from concourse.alu_op_type import AluOpType as ALU

F32 = mybir.dt.float32
I32 = mybir.dt.int32
ACT = mybir.ActivationFunctionType
AX = mybir.AxisListType

P = 128
D = 1024
S = 256
KC = D // P
ST = S // P
HEADS, DH = 8, 64
EPS = 1e-6
NEG = -1e30
WINDOWS = (2, 4, 8, 16)
BUCKETS = 32
GROUPS, PER_GROUP = 4, 8
NE = GROUPS * PER_GROUP
DE = 512
EC = DE // P
DEPTH2 = 2
LEVELS = (64, 32, 16, 8, 4, 2, 1)
NL = len(LEVELS) + 1
DFF = 4096

TILE = 2048
R = 12
T_ADA, T_IN, T_BRANCH, T_OUT = 24, 16, 4, 4
T_EXPERT = 6
T_LAYER = 12 + 4 + 16 + 16
N_TILES = T_ADA + T_IN + T_BRANCH + T_OUT + NE * T_EXPERT + DEPTH2 * T_LAYER

PRM = {}
_o = 0
for _n, _w in (("b_ada", 48), ("g1", 8), ("b_gate", 16), ("pool_scale", 4), ("g2", 8), ("gf", 8),
               ("c", 8), ("gf2", 8), ("layer", DEPTH2 * 16), ("lb_raw", DEPTH2 * 4), ("b_router", 36),
               ("w_router", 8 * 36), ("pool_w", 4 * 128)):
    PRM[_n] = (_o, _o + _w)
    _o += _w
N_PRM = _o

CST = {}
_o = 0
for _n, _w in (("ident", P), ("ones", P), ("headones", P), ("perm", P), ("invf", 1),
               ("first4", 4), ("first32", NE), ("lnmask", ST * S), ("dft_c", 2 * P),
               ("dft_t", 2 * ST * S), ("pool_a", 4 * ST * S), ("hmask", 2 * NL * P)):
    CST[_n] = (_o, _o + _w)
    _o += _w
N_CST = _o
NB_ROW = 3 * P


def constants():
    c = np.zeros((P, N_CST), np.float32)
    pos, row = np.arange(S), np.arange(P)

    def put(name, a):
        lo, hi = CST[name]
        c[:, lo:hi] = np.asarray(a, np.float64).reshape(P, hi - lo).astype(np.float32)

    put("ident", np.eye(P))
    put("ones", np.ones((P, P)))
    put("headones", (row[:, None] // DH == row[None] // DH))
    perm = np.zeros((P, P))
    for m in row:
        if m % DH < DH // 2:
            perm[m + DH // 2, m] = -1.0
        else:
            perm[m - DH // 2, m] = 1.0
    put("perm", perm)
    inv = np.float32(10000.0) ** (-np.arange(0, DH, 2, dtype=np.float32) / np.float32(DH))
    put("invf", inv[row % (DH // 2)])
    put("first4", np.broadcast_to(GROUPS - np.arange(GROUPS), (P, GROUPS)))
    put("first32", np.broadcast_to(NE - np.arange(NE), (P, NE)))
    dist = np.abs(pos[:, None] - pos[None])
    count = (dist <= 64) * 1 + (dist % 4 == 0) * 1 + (dist % 16 == 0) * 1
    ln = np.where(count > 0, np.log(np.maximum(count, 1)), NEG)
    put("lnmask", ln.reshape(ST, P, S).transpose(1, 0, 2))
    k = np.arange(DH)
    ang = 2 * np.pi * ((k[:, None] * k[None]) % DH) / DH
    blk = np.kron(np.eye(2), np.cos(ang)), np.kron(np.eye(2), np.sin(ang))
    put("dft_c", np.stack(blk, 1) / np.sqrt(DH))
    ang = 2 * np.pi * ((pos[:, None] * pos[None]) % S) / S
    dt = np.stack([np.cos(ang), -np.sin(ang)]) / np.sqrt(S)
    put("dft_t", dt.reshape(2, ST, P, S).transpose(2, 0, 1, 3))
    m = np.zeros((P, 2, NL, P))
    for n, h in enumerate(LEVELS):
        same = row[:, None] // (2 * h) == row[None] // (2 * h)
        left, right = row // h % 2 == 0, row // h % 2 == 1
        m[:, 0, n] = same & left[:, None] & right[None]
        m[:, 1, n] = same & right[:, None] & left[None]
    m[:, :, NL - 1] = np.eye(P)[:, None]
    put("hmask", m)
    a = np.zeros((4, S, S))
    for g, w in enumerate(WINDOWS):
        for t in pos:
            lo = max(t + 1 - w, 0)
            a[g, lo:t + 1, t] = 1.0 / (t + 1 - lo)
            a[g, t, t] -= 1.0
    put("pool_a", a.reshape(4, ST, P, S).transpose(2, 0, 1, 3))
    return c


def bias_table():
    m = np.arange(NB_ROW)
    n = np.maximum(m - (P - 1), 0)
    nf = np.maximum(n, 1).astype(np.float32)
    big = 16 + (np.log(nf / np.float32(16)) / np.float32(np.log(8.0)) * np.float32(16)).astype(np.int32)
    b = np.where(n < 16, n, np.minimum(big, BUCKETS - 1))
    t = np.zeros((BUCKETS + 1, NB_ROW), np.float32)
    past = m >= P - 1
    t[b[past], m[past]] = 1.0
    t[BUCKETS, ~past] = NEG
    return t


class Tok:

    def __init__(self, sem, n, loop=None, lag=0):
        self.sem, self.n, self.loop, self.lag = sem, n, loop, lag

    def before(self):
        return Tok(self.sem, self.n, self.loop, 1)


class Loop:
    def __init__(self, start, count, counted):
        self.start, self.count, self.counted, self.per = start, count, counted, {}


class Eng:

    def __init__(self, prog, name, sem):
        self.prog, self.name, self.sem, self.n = prog, name, sem, 0
        self.items = []
        self.known = {}
        self.last = None

    def need(self, *toks):
        for t in toks:
            if t is None:
                continue
            if isinstance(t, (list, tuple)):
                self.need(*t)
                continue
            key = (id(t.sem), t.lag, t.loop is not None)
            if self.known.get(key, 0) >= t.n:
                continue
            self.known[key] = t.n
            self.items.append(("wait", t))

    def op(self, fn, *needs, sig=True):
        self.need(*needs)
        if not sig:
            self.items.append(("op", fn, None))
            return None
        self.n += 1
        self.items.append(("op", fn, self.sem))
        self.last = Tok(self.sem, self.n, self.prog.loop)
        return self.last

    def raise_(self, sem, n=1):
        self.items.append(("inc", sem, n))

    def emit(self, e):
        stack = [(e, 0, None)]
        i = 0
        ctxs = []
        loop = None
        for it in self.items:
            kind = it[0]
            if kind == "wait":
                t = it[1]
                v = t.n
                if t.loop is not None and t.loop is loop:
                    per = t.loop.per.get(id(t.sem), 0)
                    if per:
                        v = t.n + (i - t.loop.start - t.lag) * per
                e.wait_ge(t.sem, v)
            elif kind == "op":
                ins = it[1](e, i)
                if it[2] is not None:
                    ins.then_inc(it[2], 1)
            elif kind == "inc":
                e.sem_inc(it[1], it[2])
            elif kind == "clear":
                e.sem_clear(it[1])
            elif kind == "loop":
                loop = it[1]
                ctx = e.Fori(loop.start, loop.start + loop.count)
                i = ctx.__enter__()
                ctxs.append(ctx)
            elif kind == "end":
                ctxs.pop().__exit__(None, None, None)
                i, loop = 0, None


class Rot:

    def __init__(self, aps):
        self.slots = [Slot(a) for a in aps]
        self.k = 0

    def take(self):
        s = self.slots[self.k % len(self.slots)]
        self.k += 1
        return s


class Slot:
    def __init__(self, ap):
        self.ap, self.free = ap, []


class Prog:
    def __init__(self, nc, ctx, dram, out):
        self.nc, self.ctx, self.dram, self.out = nc, ctx, dram, out
        self.loop = None
        sem = lambda n: ctx.enter_context(nc.semaphore(n))
        self.pe, self.act, self.dve, self.pool = (Eng(self, n, sem("done_" + n)) for n in ("pe", "act", "dve", "pool"))
        self.engs = [self.pe, self.act, self.dve, self.pool]
        self.s_slot = [sem(f"slot_filled_{i}") for i in range(R)]
        self.s_freed = sem("slots_freed")
        self.s_x, self.s_prm, self.s_cst, self.s_tab, self.s_pos = (sem(n) for n in ("x_in", "prm_in", "cst_in", "tab_in", "pos_in"))
        self.s_row, self.s_bias, self.s_out, self.s_mask = sem("bias_row_out"), sem("bias_in"), sem("result_out"), sem("mask_in")
        self.s_arrive = sem("engines_arrived")
        self.s_go = {e: sem("go_" + e.name) for e in self.engs}
        self.tile = 0
        self.to_free = 0
        fix = lambda n, cols, dt=F32: ctx.enter_context(nc.sbuf_tensor(n, [P, cols], dt))
        self.ring = [fix(f"ring{i}", TILE) for i in range(R)]
        self.x = fix("x", KC * S)
        self.h = fix("h", KC * S)
        self.prm = fix("prm", N_PRM)
        self.cst = fix("cst", CST["pool_a"][0])
        self.pool_a = fix("pool_a", 2 * NL * P)
        self.rope = fix("rope", 2 * S)
        self.small = fix("small", 256)
        self.small_used = 0
        self.cur = fix("cur", 24)
        self.base = nc.sbuf_base
        self.top = self.base
        self.bank = [ctx.enter_context(nc.psum_tensor(f"bank{i}", [P, 512], F32)) for i in range(8)]
        self.banks = Rot([b[:, :] for b in self.bank])

    def area(self, name, cols, dt=F32):
        off = (self.top + 31) // 32 * 32
        t = self.nc.alloc_sbuf_tensor_at(name, [P, cols], dt, offset=off)
        self.top = off + cols * 4
        assert self.top <= self.nc.sbuf_usable_end, (name, self.top)
        return t

    def col(self, n=1):
        a = self.small_used
        self.small_used += n
        assert self.small_used <= 256
        return self.small[:, a:a + n]

    def p(self, name, a=0, n=None):
        lo, hi = PRM[name]
        return self.prm[:, lo + a:(lo + a + n) if n is not None else hi]

    def c(self, name, a=0, n=None):
        lo, hi = CST[name]
        if name == "hmask":
            return self.pool_a[:, a:a + n]
        return self.cst[:, lo + a:(lo + a + n) if n is not None else hi]

    def next_tile(self):
        slot, fill = self.tile % R, self.tile // R + 1
        self.tile += 1
        return self.ring[slot], Tok(self.s_slot[slot], 16 * fill, self.loop)

    def done_tile(self):
        self.to_free += 1

    def mm(self, out, lhsT, rhs, start, stop, *needs, sig=False, skip=False, transpose=False):
        pe = self.pe
        if transpose:
            fn = lambda e, i: e.transpose(out, lhsT, rhs)
        else:
            fn = lambda e, i: e.matmul(out, lhsT, rhs, start=start, stop=stop, skip_group_check=skip)
        pe.need(*needs)
        if not sig and self.to_free:
            self.to_free -= 1
            pe.items.append(("op", fn, self.s_freed))
            return None
        return pe.op(fn, sig=sig)

    def flush_tiles(self):
        if self.to_free:
            self.pe.need(self.pe.last)
            self.pe.raise_(self.s_freed, self.to_free)
            self.to_free = 0

    def meet(self, clear):
        lead = self.dve
        for e in self.engs:
            e.need(e.last)
            if e is not lead:
                e.raise_(self.s_arrive)
        lead.items.append(("wait", Tok(self.s_arrive, 3)))
        if clear:
            for e in self.engs:
                lead.items.append(("clear", e.sem))
        lead.items.append(("clear", self.s_arrive))
        for e in self.engs:
            if e is not lead:
                lead.raise_(self.s_go[e])
                e.items.append(("wait", Tok(self.s_go[e], 1)))
                e.items.append(("clear", self.s_go[e]))
            if clear:
                e.n, e.last = 0, None
            e.known = {}
        for s in self.banks.slots:
            s.free = []

    def open(self, start, count, counted):
        self.loop = Loop(start, count, counted)
        self.loop0 = {e: e.n for e in self.engs}, self.tile
        for e in self.engs:
            e.items.append(("loop", self.loop))
            e.known = {}

    def close(self):
        lp = self.loop
        n0, t0 = self.loop0
        for e in self.engs:
            if lp.counted:
                per = e.n - n0[e]
                lp.per[id(e.sem)] = per
                e.n = n0[e] + per * lp.count
                if e.last is not None:
                    e.last = Tok(e.sem, e.n)
            e.items.append(("end",))
            e.known = {}
        tiles = self.tile - t0
        assert tiles % R == 0
        for s in self.s_slot:
            lp.per[id(s)] = 16 * tiles // R
        self.tile = t0 + tiles * lp.count
        self.loop = None


def linear(g, acts, toks, n_out, kc, width, evac, after=()):
    per = width // P
    for oc in range(n_out):
        if oc % per == 0:
            w, filled = g.next_tile()
        b = g.banks.take()
        j = oc % per
        for k in range(kc):
            t = g.mm(b.ap[:, 0:S], w[:, k * width + j * P:k * width + (j + 1) * P], acts[:, k, :],
                     k == 0, k == kc - 1, filled, toks[k], b.free if k == 0 else None, after, sig=(k == kc - 1))
        if j == per - 1:
            g.done_tile()
        b.free = [evac(oc, b.ap[:, 0:S], t)]


def linear_tokens(g, acts, toks, n_cols, evac):
    for j in range(n_cols // 256):
        w, filled = g.next_tile()
        for tt in range(ST):
            b = g.banks.take()
            for k in range(KC):
                t = g.mm(b.ap[:, 0:256], acts[:, k, tt * P:(tt + 1) * P], w[:, k * 256:(k + 1) * 256],
                         k == 0, k == KC - 1, filled, toks[k], b.free if k == 0 else None, sig=(k == KC - 1))
            b.free = [evac(j, tt, b.ap[:, 0:256], t)]
        g.done_tile()


def inv_rms(g, psum, out, scratch, n, t, free=()):
    a = g.dve.op(lambda e, i: e.tensor_scalar(scratch, psum, 1.0 / n, EPS, ALU.mult, ALU.add), t, *free)
    b = g.dve.op(lambda e, i: e.reciprocal(scratch, scratch), a)
    return g.act.op(lambda e, i: e.activation(out, scratch, ACT.Sqrt), b), a


def rms_norm(g, x, xt, scale, shift, h, sq, rs, scratch, after=()):
    b = g.banks.take()
    for k in range(KC):
        s = g.act.op(lambda e, i, k=k: e.activation(sq[:, k, :], x[:, k, :], ACT.Square), xt[k], *after)
        t = g.mm(b.ap[:, 0:S], g.c("ones"), sq[:, k, :], k == 0, k == KC - 1, s, b.free if k == 0 else None,
                 sig=(k == KC - 1))
    r, read = inv_rms(g, b.ap[:, 0:S], rs, scratch, D, t)
    b.free = [read]
    toks = []
    for k in range(KC):
        a = g.dve.op(lambda e, i, k=k: e.scalar_tensor_tensor(out=h[:, k, :], in0=x[:, k, :], scalar=scale[:, k:k + 1],
                                                              in1=rs, op0=ALU.mult, op1=ALU.mult), r, xt[k], *after)
        if shift is not None:
            a = g.act.op(lambda e, i, k=k: e.activation(h[:, k, :], h[:, k, :], ACT.Identity, bias=shift[:, k:k + 1]), a)
        toks.append(a)
    return toks


def attention(g, q, k, v, qk_toks, v_toks, add, add_tok, causal, out, pbuf, ptbuf, name):
    state = {}
    out_toks = []

    def scores(c):
        for j in range(2):
            for qt in range(ST):
                hd, lo = 2 * c + j, DH * j
                nk = (qt + 1) * P if causal else S
                b, pb = g.banks.take(), pbuf.take()
                t = g.mm(b.ap[:, 0:nk], q[lo:lo + DH, c, qt * P:(qt + 1) * P], k[lo:lo + DH, c, 0:nk],
                         True, True, qk_toks[c], b.free, sig=True)
                m, s = g.col(), g.col()
                pr = pb.ap[:, 0:nk]
                a = g.dve.op(lambda e, i, pr=pr, b=b, nk=nk, hd=hd, qt=qt: e.scalar_tensor_tensor(
                    out=pr, in0=b.ap[:, 0:nk], scalar=DH ** -0.5, in1=add(hd, qt), op0=ALU.mult, op1=ALU.add),
                    t, add_tok, pb.free)
                b.free = [a]
                a = g.dve.op(lambda e, i, m=m, pr=pr: e.tensor_reduce(m, pr, AX.X, ALU.max, negate=True), a)
                a = g.act.op(lambda e, i, m=m, s=s, pr=pr: e.activation(pr, pr, ACT.Exp, bias=m, accum_out=s), a)
                a = g.dve.op(lambda e, i, s=s: e.reciprocal(s, s), a)
                a = g.dve.op(lambda e, i, s=s, pr=pr: e.tensor_scalar(pr, pr, s, None, ALU.mult), a)
                state[c, j, qt] = pb, a

    def turn(c):
        for j in range(2):
            b, pt = g.banks.take(), ptbuf.take()
            pieces = [(kt, qt) for kt in range(ST) for qt in range(ST) if not (causal and kt > qt)]
            for n, (kt, qt) in enumerate(pieces):
                pb, a = state[c, j, qt]
                t = g.mm(b.ap[:, n * P:(n + 1) * P], pb.ap[:, kt * P:(kt + 1) * P], g.c("ident"), True, True,
                         a, b.free, sig=True, transpose=True)
            for qt in range(ST):
                state[c, j, qt][0].free = [t]
            w = len(pieces) * P
            a = g.act.op(lambda e, i, pt=pt, b=b, w=w: e.copy(pt.ap[:, 0:w], b.ap[:, 0:w]), t, pt.free)
            b.free = [a]
            state[c, j] = pt, a

    def mix(c):
        b = g.banks.take()
        for j in range(2):
            pt, a = state[c, j]
            hd, lo = 2 * c + j, DH * j
            w = S if not causal else P
            g.mm(b.ap[lo:lo + DH, 0:S], v[:, 0, hd * DH:(hd + 1) * DH], pt.ap[:, 0:S], True, False,
                 a, v_toks, b.free)
            t = g.mm(b.ap[lo:lo + DH, S - w:S], v[:, 1, hd * DH:(hd + 1) * DH], pt.ap[:, S:S + w], False, True, sig=True)
            pt.free = [t]
        a = g.act.op(lambda e, i, b=b: e.copy(out[:, c, :], b.ap[:, 0:S]), t)
        b.free = [a]
        out_toks.append(a)

    n = HEADS // 2
    for c in range(n + 2):
        if c < n:
            scores(c)
        if 1 <= c <= n:
            turn(c - 1)
        if c >= 2:
            mix(c - 2)
    return out_toks


def first_block(g, xt):
    pe, act, dve, pool = g.pe, g.act, g.dve, g.pool
    g.top = g.base
    x, h = (t[:, :].rearrange("p (k t) -> p k t", k=KC) for t in (g.x, g.h))
    prm, cst = g.t_prm, g.t_cst
    pool_a = g.pool_a
    bias = g.area("bias", HEADS * 384)
    g.bias = bias
    q = g.area("q1", 4 * S)
    k_off = g.top
    k, u, v = (g.area(n, 4 * S) for n in ("k1", "u1", "v1"))
    q3, k3 = (t[:, :].rearrange("p (c t) -> p c t", c=4) for t in (q, k))
    v3, u3 = (t[:, :].rearrange("p (s f) -> p s f", s=ST) for t in (v, u))
    gate = g.area("gate", 16 * S)
    gate3 = gate[:, :].rearrange("p (c t) -> p c t", c=16)
    att = g.area("att1", 4 * S)[:, :].rearrange("p (c t) -> p c t", c=4)
    pol = q3
    pbuf = Rot([g.area(f"p1_{i}", S)[:, :] for i in range(8)])
    ptbuf = Rot([g.area(f"pt1_{i}", 2 * S)[:, :] for i in range(4)])
    rs, scr = g.area("rs1", S)[:, :], g.area("scr1", S)[:, :]
    mod = g.area("mod", 48)
    mod1 = g.area("mod1", 48)
    cact, sc1, sc2 = (g.area(n, KC) for n in ("cact", "sc1", "sc2"))
    g.rb = g.area("rb", 8)
    g.tab, g.row, g.tab_neg = (gate[:, 2048 + n * NB_ROW:2048 + (n + 1) * NB_ROW] for n in range(3))

    ca = act.op(lambda e, i: e.activation(cact[:, :], g.p("c"), ACT.Silu), prm)

    b = g.banks.take()
    t = g.mm(b.ap[0:HEADS, 0:NB_ROW], g.rb[0:BUCKETS, 0:HEADS], g.tab[0:BUCKETS, :], True, True, g.t_tab, sig=True)
    a = dve.op(lambda e, i, b=b: e.tensor_tensor(g.row[0:HEADS, :], b.ap[0:HEADS, 0:NB_ROW], g.tab_neg[0:HEADS, :], ALU.add), t, g.t_tab)
    b.free = [a]
    g.t_row = a
    bias_tok = Tok(g.s_bias, 32)

    def add(hd, qt):
        o = hd * P if qt == 0 else HEADS * P + hd * S
        nk = (qt + 1) * P
        return bias[:, o:o + nk][:, ::-1]

    def ada(n_tiles, bank, col0):
        t = None
        for n in range(n_tiles):
            w, filled = g.next_tile()
            for j in range(2):
                for kk in range(KC):
                    last = kk == KC - 1
                    t = g.mm(bank.ap[:, 2 * n + j:2 * n + j + 1], w[:, kk * 256 + j * P:kk * 256 + (j + 1) * P],
                             cact[:, kk:kk + 1], kk == 0, last, filled, ca, bank.free if n + j + kk == 0 else None, sig=last)
            g.done_tile()
        m = 2 * n_tiles
        a = dve.op(lambda e, i: e.tensor_tensor(mod[:, col0:col0 + m], bank.ap[:, 0:m], g.p("b_ada", col0, m), ALU.add), t)
        bank.free = [a]
        return dve.op(lambda e, i: e.tensor_scalar(mod1[:, col0:col0 + m], mod[:, col0:col0 + m], 1.0, None, ALU.add), a)

    a = ada(8, g.banks.take(), 0)
    a = dve.op(lambda e, i: e.tensor_tensor(sc1[:, :], mod1[:, 8:16], g.p("g1"), ALU.mult), a)
    sq = gate[:, 0:KC * S].rearrange("p (k t) -> p k t", k=KC)
    ht = rms_norm(g, x, xt, sc1[:, :], mod[:, 0:8], h, sq, rs, scr, after=(a,))

    qk = []
    def ev_qk(oc, ps, t):
        dst = (q3 if oc < 4 else k3)[:, oc % 4, :]
        a = act.op(lambda e, i: e.copy(dst, ps), t)
        qk.append(a)
        return a
    linear(g, h, ht, 8, KC, 256, ev_qk)
    vt, ut = [], []
    def ev_vu(j, tt, ps, t):
        dst = (v3 if j < 2 else u3)[:, tt, (j % 2) * 256:(j % 2 + 1) * 256]
        a = dve.op(lambda e, i: e.tensor_copy(dst, ps), t)
        (vt if j < 2 else ut).append(a)
        return a
    linear_tokens(g, h, ht, 1024, ev_vu)
    att_t = attention(g, q3, k3, v3, [[qk[c], qk[4 + c]] for c in range(4)], vt, add, bias_tok, True, att, pbuf, ptbuf, "a")

    gt = []
    act.need(Tok(g.s_row, 16))
    def ev_gate(oc, ps, t):
        a = act.op(lambda e, i: e.activation(gate3[:, oc, :], ps, ACT.Sigmoid, bias=g.p("b_gate", oc, 1)), t)
        gt.append(a)
        return a
    linear(g, h, ht, 16, KC, 256, ev_gate)

    pol_t = []
    for gr in range(4):
        b = g.banks.take()
        for tt in range(ST):
            o = (gr * ST + tt) * S
            t = g.mm(b.ap[:, 0:S], u3[:, tt, gr * P:(gr + 1) * P], pool_a[:, o:o + S], tt == 0, tt == ST - 1,
                     ut, g.t_pool_a, b.free, sig=(tt == ST - 1))
        dif = pbuf.take()
        a = act.op(lambda e, i, b=b, dif=dif: e.copy(dif.ap, b.ap[:, 0:S]), t, dif.free)
        b.free = [a]
        b2 = g.banks.take()
        t = g.mm(b2.ap[:, 0:S], g.p("pool_w", gr * P, P), dif.ap, True, True, a, b2.free, sig=True)
        dif.free = [t]
        a = act.op(lambda e, i, b=b2, gr=gr: e.mul(pol[:, gr, :], b.ap[:, 0:S], g.p("pool_scale", gr, 1)), t, att_t[-1])
        b2.free = [a]
        pol_t.append(a)
    g.t_pooled = t

    ada_t = ada(16, g.banks.take(), 16)

    mixed = h
    h_read = pe.last
    mt = [None] * KC
    def ev_attn(oc, ps, t):
        mt[oc] = dve.op(lambda e, i: e.tensor_tensor(mixed[:, oc, :], gate3[:, oc, :], ps, ALU.mult), t, gt, h_read)
        return mt[oc]
    linear(g, att, att_t, KC, 4, 512, ev_attn)
    def ev_pool(oc, ps, t):
        a = dve.op(lambda e, i: e.tensor_tensor(gate3[:, 8 + oc, :], gate3[:, 8 + oc, :], ps, ALU.mult), t)
        mt[oc] = dve.op(lambda e, i: e.tensor_tensor(mixed[:, oc, :], mixed[:, oc, :], gate3[:, 8 + oc, :], ALU.add), a)
        return a
    linear(g, pol, pol_t, KC, 4, 512, ev_pool)
    def ev_out(oc, ps, t):
        xt[oc] = dve.op(lambda e, i: e.scalar_tensor_tensor(out=x[:, oc, :], in0=ps, scalar=mod[:, 16 + oc:17 + oc],
                                                            in1=x[:, oc, :], op0=ALU.mult, op1=ALU.add), t, ada_t)
        return xt[oc]
    linear(g, mixed, mt, KC, KC, 256, ev_out)

    a = dve.op(lambda e, i: e.tensor_tensor(sc2[:, :], mod1[:, 32:40], g.p("g2"), ALU.mult), ada_t)
    ht = rms_norm(g, x, xt, sc2[:, :], mod[:, 24:32], h, sq, rs, scr, after=(a, pe.last))
    g.top = k_off
    comb = route(g, h, ht)
    g.flush_tiles()
    experts(g, h, ht, comb, gate, pbuf, ptbuf)
    toks = []
    for k in range(KC):
        ps = g.bank[4 + k // 2][:, (k % 2) * S:(k % 2 + 1) * S]
        toks.append(dve.op(lambda e, i, k=k, ps=ps: e.scalar_tensor_tensor(
            out=x[:, k, :], in0=ps, scalar=mod[:, 40 + k:41 + k], in1=x[:, k, :], op0=ALU.mult, op1=ALU.add), pe.last))
    for s in g.banks.slots[4:]:
        s.free = [toks[-1]]
    ht = rms_norm(g, x, toks, g.p("gf"), None, x, sq, rs, scr)
    return ht


def route(g, h, ht):
    dve, act = g.dve, g.act
    z = g.area("z", ST * 36)[:, :].rearrange("p (s f) -> p s f", s=ST)
    comb = g.area("comb", ST * NE)
    sel, one, tmp = (g.area(n, ST * NE) for n in ("rt_sel", "rt_one", "rt_tmp"))
    v4 = lambda a: a[:, :].rearrange("p (s n e) -> p s n e", s=ST, n=GROUPS)
    v3 = lambda a: a[:, :].rearrange("p (s e) -> p s e", s=ST)
    gr, goh = g.area("rt_g", ST * GROUPS), g.area("rt_goh", ST * GROUPS)
    g3, goh3 = (a[:, :].rearrange("p (s n) -> p s n", s=ST) for a in (gr, goh))
    ms = g.area("rt_m", 16 * ST)
    cnt = [0]

    def stat():
        cnt[0] += 1
        return ms[:, (cnt[0] - 1) * ST:cnt[0] * ST]

    def bc(a, n):
        return a.unsqueeze(2).to_broadcast([P, ST, n])

    t = None
    chain = [None]

    def d(fn, *needs):
        chain[0] = dve.op(fn, chain[0], *needs)
        return chain[0]

    for tt in range(ST):
        b = g.banks.take()
        for k in range(KC):
            t = g.mm(b.ap[:, 0:36], h[:, k, tt * P:(tt + 1) * P], g.p("w_router", k * 36, 36), k == 0, k == KC - 1,
                     ht[k], b.free, sig=(k == KC - 1))
        a = d(lambda e, i, b=b, tt=tt: e.tensor_tensor(z[:, tt, :], b.ap[:, 0:36], g.p("b_router"), ALU.add), t)
        b.free = [a]
    zg = z[:, :, 0:GROUPS]
    m, s, e1 = stat(), stat(), stat()
    first4 = g.c("first4").unsqueeze(1).to_broadcast([P, ST, GROUPS])
    first32 = g.c("first32").unsqueeze(1).to_broadcast([P, ST, NE])
    d(lambda e, i: e.tensor_reduce(m, zg, AX.X, ALU.max))
    d(lambda e, i: e.tensor_tensor(goh3, zg, bc(m, GROUPS), ALU.is_equal))
    d(lambda e, i: e.tensor_tensor(goh3, goh3, first4, ALU.mult))
    d(lambda e, i: e.tensor_reduce(e1, goh3, AX.X, ALU.max))
    d(lambda e, i: e.tensor_tensor(goh3, goh3, bc(e1, GROUPS), ALU.is_equal))
    a = d(lambda e, i: e.tensor_tensor(g3, zg, bc(m, GROUPS), ALU.subtract))
    a = act.op(lambda e, i: e.activation(gr[:, :], gr[:, :], ACT.Exp), a)
    pg = stat()
    d(lambda e, i: e.tensor_reduce(s, g3, AX.X, ALU.add), a)
    d(lambda e, i: e.reciprocal(pg, s))
    oh4 = goh3.unsqueeze(3).to_broadcast([P, ST, GROUPS, PER_GROUP])
    one4 = v4(one)
    for tt in range(ST):
        zt = z[:, tt, GROUPS:36].rearrange("p (n e) -> p n e", n=GROUPS)
        d(lambda e, i, tt=tt, zt=zt: e.tensor_tensor(v4(sel)[:, tt], zt, oh4[:, tt], ALU.mult))
        d(lambda e, i, tt=tt: e.tensor_scalar(one4[:, tt], oh4[:, tt], 1.0, -NEG, ALU.subtract, ALU.mult))
    d(lambda e, i: e.tensor_tensor(sel[:, :], sel[:, :], one[:, :], ALU.add))
    tops = []
    for n in range(2):
        mm_, fi = stat(), stat()
        oh = (one, tmp)[n]
        d(lambda e, i, mm_=mm_: e.tensor_reduce(mm_, v3(sel), AX.X, ALU.max))
        d(lambda e, i, mm_=mm_, oh=oh: e.tensor_tensor(v3(oh), v3(sel), bc(mm_, NE), ALU.is_equal))
        d(lambda e, i, oh=oh: e.tensor_tensor(v3(oh), v3(oh), first32, ALU.mult))
        d(lambda e, i, fi=fi, oh=oh: e.tensor_reduce(fi, v3(oh), AX.X, ALU.max))
        d(lambda e, i, fi=fi, oh=oh: e.tensor_tensor(v3(oh), v3(oh), bc(fi, NE), ALU.is_equal))
        if n == 0:
            d(lambda e, i, oh=oh: e.scalar_tensor_tensor(out=sel[:, :], in0=oh[:, :], scalar=3 * NEG, in1=sel[:, :],
                                                         op0=ALU.mult, op1=ALU.add))
        tops.append(mm_)
    df, w1, w2 = stat(), stat(), stat()
    a = d(lambda e, i: e.tensor_tensor(df, tops[1], tops[0], ALU.subtract))
    a = act.op(lambda e, i: e.activation(df, df, ACT.Exp), a)
    d(lambda e, i: e.tensor_scalar(w1, df, 1.0, None, ALU.add), a)
    d(lambda e, i: e.reciprocal(w1, w1))
    d(lambda e, i: e.tensor_tensor(w1, w1, pg, ALU.mult))
    d(lambda e, i: e.tensor_tensor(w2, w1, df, ALU.mult))
    d(lambda e, i: e.tensor_tensor(v3(one), v3(one), bc(w1, NE), ALU.mult))
    d(lambda e, i: e.tensor_tensor(v3(tmp), v3(tmp), bc(w2, NE), ALU.mult))
    g.t_comb = chain[0]
    g.t_comb = d(lambda e, i: e.tensor_tensor(comb[:, :], one[:, :], tmp[:, :], ALU.add))
    g.comb = comb
    g.picked = one, tmp
    return comb


def experts(g, h, ht, comb, work, pbuf, ptbuf):
    pe, act, dve = g.pe, g.act, g.dve
    acts = [g.gate_area(work, n) for n in range(2)]
    diag = work[:, 3072:3072 + 2 * P]
    cbs = work[:, 3328:3328 + 2 * S]
    zero = g.area("zero", 512)
    zt = dve.op(lambda e, i: e.memset(zero[:, :], 0.0))
    for n in range(4):
        t = g.mm(g.bank[4 + n][:, :], zero[:, 0:P], zero[:, :], True, True, zt, g.banks.slots[4 + n].free, sig=True)
    all_free = [s.free for s in g.banks.slots[:4]]
    g.meet(clear=False)
    g.open(0, NE // 2, counted=True)
    banks = [g.bank[n][:, :] for n in range(4)]
    comb3 = comb[:, :].rearrange("p (s e) -> p s e", s=ST)
    prev = {}
    last = {}
    pend = []

    def wait_prev(key):
        t = last.get(key)
        return t

    bank_k = [0]
    bank_reader = {}
    first_wait = []

    def take():
        n = bank_k[0] % 4
        bank_k[0] += 1
        if n not in bank_reader:
            holder = []
            first_wait.append((n, holder))
            return n, holder
        return n, [bank_reader[n]]

    act_reader = {}
    for ex in range(2):
        A = acts[ex]
        n, free = take()
        cb_b = n
        if ex in (0, 1):
            hold_cb = []
            first_wait.append((("cb", ex), hold_cb))
        tds = []
        for tt in range(ST):
            tds.append(dve.op(lambda e, i, tt=tt, ex=ex: e.tensor_scalar(
                diag[:, tt * P:(tt + 1) * P], g.c("ident"), comb3[:, tt, bass.ds(i * 2 + ex, 1)], None, ALU.mult),
                *( [act_reader["diag"]] if "diag" in act_reader else [])))
        if "diag0" not in act_reader:
            act_reader["diag0"] = True
        pe.items.append(("hold", free))
        for tt in range(ST):
            t = g.mm(banks[n][:, tt * P:(tt + 1) * P], g.c("ones"), diag[:, tt * P:(tt + 1) * P], True, True, tds[tt], sig=True)
        act_reader["diag"] = t
        cb = cbs[:, ex * S:(ex + 1) * S]
        act.items.append(("hold", hold_cb))
        a_cb = act.op(lambda e, i, n=n, cb=cb: e.copy(cb, banks[n][:, 0:S]), t)
        bank_reader[n] = a_cb
        a_toks = []
        for half in range(2):
            wg, fg = g.next_tile()
            wu, fu = g.next_tile()
            for j in range(2):
                pair = []
                for w, f in ((wg, fg), (wu, fu)):
                    n, free = take()
                    pe.items.append(("hold", free))
                    for k in range(KC):
                        t = g.mm(banks[n][:, 0:S], w[:, k * 256 + j * P:k * 256 + (j + 1) * P], h[:, k, :],
                                 k == 0, k == KC - 1, f, sig=(k == KC - 1))
                    if j == 1:
                        g.done_tile()
                    pair.append((n, t))
                fc = 2 * half + j
                (ng, tg), (nu, tu) = pair
                hold_a = []
                first_wait.append((("act", ex), hold_a))
                act.items.append(("hold", hold_a))
                a = act.op(lambda e, i, A=A, fc=fc, n=ng: e.activation(A[:, fc, :], banks[n][:, 0:S], ACT.Silu), tg)
                bank_reader[ng] = a
                a = dve.op(lambda e, i, A=A, fc=fc, n=nu: e.tensor_tensor(A[:, fc, :], A[:, fc, :], banks[n][:, 0:S], ALU.mult), a, tu)
                bank_reader[nu] = a
                a_toks.append(dve.op(lambda e, i, A=A, fc=fc, cb=cb: e.tensor_tensor(A[:, fc, :], A[:, fc, :], cb, ALU.mult), a, a_cb))
        pend.append((A, a_toks))
        for half in range(2):
            w, f = g.next_tile()
            for j in range(4):
                oc = 4 * half + j
                for k in range(EC):
                    t = g.mm(g.bank[4 + oc // 2][:, (oc % 2) * S:(oc % 2 + 1) * S],
                             w[:, k * 512 + j * P:k * 512 + (j + 1) * P], A[:, k, :], False, False, f, a_toks[k],
                             sig=(k == EC - 1 and j == 3), skip=True)
            g.done_tile()
        last["act", ex] = t
        last["cb", ex] = a_toks[-1]
        g.flush_tiles()
    for key, holder in first_wait:
        if isinstance(key, int):
            holder.append(bank_reader[key].before())
        elif key[0] == "act":
            holder.append(last[key].before())
        else:
            holder.append(last[key].before())
    g.fix_holds()
    g.close()
    g.banks.k = 0
    for s in g.banks.slots:
        s.free = []
    g.meet(clear=False)


def second_consts(g):
    act, dve = g.act, g.dve
    g.top = g.base
    ang, kf, r, r2 = (g.area(n, S)[:, :] for n in ("ang", "kf", "r", "r2"))
    ki = g.area("ki", S, I32)[:, :]
    posi = g.posi
    two_pi = 2 * np.pi
    c1 = 6.28125
    c2 = float(np.float32(np.float32(two_pi - c1).view(np.uint32) & np.uint32(0xFFFFF000)).astype(np.float32)) if False else 0.0019350051879882812
    c3 = two_pi - c1 - c2
    pi = float(np.nextafter(np.float32(np.pi), np.float32(0)))
    ch = [None]

    def d(fn, *needs):
        ch[0] = dve.op(fn, ch[0], *needs)
        return ch[0]

    d(lambda e, i: e.tensor_copy(ang, posi[:, :]), g.t_pos)
    d(lambda e, i: e.tensor_scalar(ang, ang, g.c("invf"), None, ALU.mult), g.t_cst)
    d(lambda e, i: e.tensor_scalar(kf, ang, 1.0 / two_pi, None, ALU.mult))
    d(lambda e, i: e.tensor_copy(ki, kf))
    d(lambda e, i: e.tensor_copy(kf, ki))
    d(lambda e, i: e.scalar_tensor_tensor(out=r, in0=kf, scalar=-c1, in1=ang, op0=ALU.mult, op1=ALU.add))
    d(lambda e, i: e.scalar_tensor_tensor(out=r, in0=kf, scalar=-c2, in1=r, op0=ALU.mult, op1=ALU.add))
    d(lambda e, i: e.scalar_tensor_tensor(out=r, in0=kf, scalar=-c3, in1=r, op0=ALU.mult, op1=ALU.add))
    d(lambda e, i: e.tensor_scalar(r2, r, np.pi / 2, None, ALU.add))
    d(lambda e, i: e.tensor_scalar(kf, r2, np.pi, -two_pi, ALU.is_gt, ALU.mult))
    d(lambda e, i: e.tensor_tensor(r2, r2, kf, ALU.add))
    for a in (r, r2):
        t = d(lambda e, i, a=a: e.tensor_scalar(a, a, pi, -pi, ALU.min, ALU.max))
    cos, sin = g.rope[:, 0:S], g.rope[:, S:2 * S]
    act.op(lambda e, i: e.activation(cos, r2, ACT.Sin), t)
    g.t_rope = act.op(lambda e, i: e.activation(sin, r, ACT.Sin), t)
    lb = g.lb
    raw = g.p("lb_raw")
    m, e0, s = g.area("lb_m", 4)[:, :], g.area("lb_e", 8), g.area("lb_s", 4)[:, :]
    d(lambda e, i: e.tensor_tensor(m, raw[:, 0:4], raw[:, 4:8], ALU.max), g.t_prm)
    d(lambda e, i: e.tensor_tensor(e0[:, 0:4], raw[:, 0:4], m, ALU.subtract))
    t = d(lambda e, i: e.tensor_tensor(e0[:, 4:8], raw[:, 4:8], m, ALU.subtract))
    t = act.op(lambda e, i: e.activation(e0[:, :], e0[:, :], ACT.Exp), t)
    d(lambda e, i: e.tensor_tensor(s, e0[:, 0:4], e0[:, 4:8], ALU.add), t)
    d(lambda e, i: e.reciprocal(s, s))
    for l in range(2):
        d(lambda e, i, l=l: e.tensor_tensor(e0[:, 4 * l:4 * l + 4], e0[:, 4 * l:4 * l + 4], s, ALU.mult))
    d(lambda e, i: e.tensor_tensor(lb[:, 0:4], e0[:, 0:4], e0[:, 0:4], ALU.subtract))
    d(lambda e, i: e.tensor_tensor(m, e0[:, 0:4], e0[:, 4:8], ALU.add))
    d(lambda e, i: e.tensor_tensor(lb[:, 8:12], m, e0[:, 0:4], ALU.subtract))
    for l in range(2):
        t = d(lambda e, i, l=l: e.tensor_scalar(lb[:, 8 * l + 4:8 * l + 8], lb[:, 8 * l:8 * l + 4], -1.0, 1.0, ALU.mult, ALU.add))
    return t


def second_layer(g):
    pe, act, dve, pool = g.pe, g.act, g.dve, g.pool
    g.top = g.base
    x, h = (t[:, :].rearrange("p (k t) -> p k t", k=KC) for t in (g.x, g.h))
    chunked = lambda name, n: g.area(name, n * S)[:, :].rearrange("p (c t) -> p c t", c=n)
    sq = chunked("sq2", 8)
    rs, scr = g.area("rs2", S)[:, :], g.area("scr2", S)[:, :]
    q, sg, kk, cum = chunked("aq", 2), chunked("sg", 4), chunked("kk", 4), chunked("cum", 4)
    gsil = chunked("gs", 2)
    av, cv = (g.area(n, ST * w)[:, :].rearrange("p (s f) -> p s f", s=ST) for n, w in (("av", 256), ("cv", 512)))
    uT = chunked("uT", 2)
    cq, ck = chunked("cq", 4), chunked("ck", 4)
    mixed = chunked("mixed", 8)
    lead = g.c("ones", 0, 1).to_broadcast([P, S])
    cur = g.cur

    l0 = PRM["layer"][0]
    a = dve.op(lambda e, i: e.tensor_copy(cur[:, 0:16], g.prm[:, bass.ds(i * 16 + l0, 16)]))
    ct = dve.op(lambda e, i: e.tensor_copy(cur[:, 16:24], g.lb[:, bass.ds(i * 8, 8)]))
    ht = rms_norm(g, x, [None] * KC, cur[:, 0:8], None, h, sq, rs, scr, after=(a, ct))

    T = {}
    def ev(oc, ps, t):
        if oc < 2:
            a = act.op(lambda e, i: e.activation(q[:, oc, :], ps, ACT.Silu), t)
            T["q", oc] = a
        elif oc < 4:
            a = act.op(lambda e, i: e.activation(gsil[:, oc - 2, :], ps, ACT.Silu), t)
            T["g", oc - 2] = a
        elif oc < 8:
            n = oc - 4
            a = act.op(lambda e, i: e.activation(sg[:, n, :], ps, ACT.Sigmoid), t)
            f = dve.op(lambda e, i: e.tensor_scalar(sg[:, n, :], sg[:, n, :], cur[:, 20 + n:21 + n], cur[:, 16 + n:17 + n],
                                                    ALU.mult, ALU.add), a, ct)
            T["k", n] = dve.op(lambda e, i: e.tensor_scalar(kk[:, n, :], sg[:, n, :], -1.0, 1.0, ALU.mult, ALU.add), f)
            T["f", n] = dve.op(lambda e, i: e.tensor_scalar(sg[:, n, :], sg[:, n, :], 2.0 ** -64, None, ALU.max), T["k", n])
        elif oc < 10:
            a = dve.op(lambda e, i: e.tensor_copy(uT[:, oc - 8, :], ps), t)
            T["u", oc - 8] = a
        else:
            n = oc - 10
            dst = (cq if n < 4 else ck)[:, n % 4, :]
            a = act.op(lambda e, i: e.copy(dst, ps), t)
            T["c", n] = a
        return a
    linear(g, h, ht, 18, KC, 256, ev)
    vt = []
    def ev_v(j, tt, ps, t):
        dst = av[:, tt, :] if j == 0 else cv[:, tt, (j - 1) * 256:j * 256]
        a = dve.op(lambda e, i: e.tensor_copy(dst, ps), t)
        vt.append((j, a))
        return a
    linear_tokens(g, h, ht, 768, ev_v)
    avt, cvt = [a for j, a in vt if j == 0], [a for j, a in vt if j > 0]

    a = act.op(lambda e, i: e.activation(sg, sg, ACT.Ln), *[T["f", n] for n in range(4)])
    for n in range(4):
        rev = slice(None, None, -1) if n >= 2 else slice(None)
        T["b", n] = dve.op(lambda e, i, n=n, rev=rev: e.tensor_tensor_scan(
            out=cum[:, n, rev], data0=lead, data1=sg[:, n, rev], initial=0.0, op0=ALU.mult, op1=ALU.add), a)

    mt = [None] * KC
    hgrn(g, T, q, kk, cum, gsil, av, avt, mixed, mt, sq)
    fourier(g, T, uT, cum, mixed, mt)

    base = g.top
    rots = Rot([kk[:, 0:2, :], kk[:, 2:4, :]])
    cos, sin = (g.rope[:, o:o + S].unsqueeze(1).to_broadcast([P, 2, S]) for o in (0, S))
    qk_t = []
    for n in range(8):
        src = (cq if n < 4 else ck)
        if n % 2 == 0:
            b = g.banks.take()
        t = g.mm(b.ap[:, (n % 2) * S:(n % 2 + 1) * S], g.c("perm"), src[:, n % 4, :], True, True, T["c", n],
                 b.free if n % 2 == 0 else None, sig=True)
        if n % 2 == 1:
            c = n % 4
            s2 = src[:, c - 1:c + 1, :]
            rt = rots.take()
            r2 = rt.ap
            a = dve.op(lambda e, i, b=b, r2=r2: e.tensor_tensor(r2, b.ap[:, :].rearrange("p (c t) -> p c t", c=2), sin, ALU.mult), t, g.hgrn_read)
            b.free = [a]
            a2 = dve.op(lambda e, i, s2=s2: e.tensor_tensor(s2, s2, cos, ALU.mult), t)
            a = dve.op(lambda e, i, s2=s2, r2=r2: e.tensor_tensor(s2, s2, r2, ALU.add), a, a2)
            qk_t += [a, a]
    pbuf = Rot([g.m_all[:, i * S:(i + 1) * S] for i in range(8)])
    ptbuf = Rot([g.m_all[:, (8 + 2 * i) * S:(10 + 2 * i) * S] for i in range(4)])
    for b in pbuf.slots + ptbuf.slots:
        b.free = [g.hgrn_read]
    att = mixed[:, 4:8, :]
    g.small_used = 0
    at = attention(g, cq, ck, cv, [[qk_t[c], qk_t[4 + c]] for c in range(4)], cvt,
                   lambda hd, qt: g.c("lnmask", qt * S, S), None, False, att, pbuf, ptbuf, "b")
    mt[4:8] = at

    xt = [None] * KC
    def ev_out(oc, ps, t):
        xt[oc] = dve.op(lambda e, i: e.tensor_tensor(x[:, oc, :], x[:, oc, :], ps, ALU.add), t)
        return xt[oc]
    linear(g, mixed, mt, KC, KC, 256, ev_out)

    g.top = g.base
    sq_, rs_, scr_ = sq, rs, scr
    g.top = g.base + 4 * (8 * S + 2 * S) + 256
    hid = g.area("hid", 32 * S)[:, :].rearrange("p (c t) -> p c t", c=32)
    over = (pe.last, dve.last, act.last, xt[-1])
    ht = rms_norm(g, x, xt, cur[:, 8:16], None, h, sq, rs, scr, after=(pe.last,))
    hd = []
    def ev_up(oc, ps, t):
        a = act.op(lambda e, i: e.activation(hid[:, oc, :], ps, ACT.Relu), t, *over)
        hd.append(dve.op(lambda e, i: e.tensor_tensor(hid[:, oc, :], hid[:, oc, :], hid[:, oc, :], ALU.mult), a))
        return a
    linear(g, h, ht, 32, KC, 256, ev_up)
    for oc in range(KC):
        b = g.banks.take()
        for half in range(2):
            w, f = g.next_tile()
            for k in range(16):
                fc = half * 16 + k
                t = g.mm(b.ap[:, 0:S], w[:, k * P:(k + 1) * P], hid[:, fc, :], fc == 0, fc == 31, f, hd[fc],
                         b.free if fc == 0 else None, sig=(fc == 31))
            g.done_tile()
        a = dve.op(lambda e, i, b=b, oc=oc: e.tensor_tensor(x[:, oc, :], x[:, oc, :], b.ap[:, 0:S], ALU.add), t)
        b.free = [a]
    g.flush_tiles()


def hgrn(g, T, q, kk, cum, gsil, av, avt, mixed, mt, sq):
    pe, act, dve = g.pe, g.act, g.dve
    n_lv = len(LEVELS) + 1
    M = []
    ex = [g.h[:, n * 4 * S:(n + 1) * 4 * S].rearrange("p (c t) -> p c t", c=4) for n in range(2)]
    ex_free = [[pe.last], [pe.last]]
    m_all = g.area("hm", n_lv * 2 * S)
    Mb = [m_all[:, n * 2 * S:(n + 1) * 2 * S].rearrange("p (c t) -> p c t", c=2) for n in range(n_lv)]
    g.m_all = m_all
    AT = sq[:, :, :].rearrange("p h t -> p (h t)").rearrange("p (h f) -> p h f", h=8)
    AL = g.area("hal", 8 * P)[:, :].rearrange("p (h f) -> p h f", h=8)
    tmp = mixed[:, 4:8, :].rearrange("p c t -> p (c t)")
    tmp_free = []
    at = {}
    m_free = []
    k_uses = 0
    for dr in range(2):
        M = []
        for lv, hh in enumerate((128,) + LEVELS):
            X, m = ex[k_uses % 2][:, 0:2, :], Mb[lv]
            xf = ex_free[k_uses % 2]
            nb = 2 * S // (2 * hh)
            split = lambda a, hh=hh: a.rearrange("p c (n s h) -> p (c n) s h", s=2, h=hh)
            cv = split(cum[:, 2 * dr:2 * dr + 2, :])
            mid = (cv[:, :, 0, hh - 1:hh] if dr == 0 else cv[:, :, 1, 0:1]).to_broadcast([P, nb, hh])
            subs = []
            for side in range(2):
                is_q = (side == 1) == (dr == 0)
                o, b_ = split(X)[:, :, side, :], cv[:, :, side, :]
                a0, a1 = (b_, mid) if is_q else (mid, b_)
                subs.append(dve.op(lambda e, i, o=o, a0=a0, a1=a1: e.tensor_tensor(o, a0, a1, ALU.subtract),
                                   T["b", 2 * dr], T["b", 2 * dr + 1], xf))
            a = act.op(lambda e, i, X=X: e.activation(X, X, ACT.Exp), *subs)
            for side in range(2):
                is_q = (side == 1) == (dr == 0)
                src = q if is_q else kk[:, 2 * dr:2 * dr + 2, :]
                o, xx, sv = split(m)[:, :, side, :], split(X)[:, :, side, :], split(src)[:, :, side, :]
                t = dve.op(lambda e, i, o=o, xx=xx, sv=sv: e.tensor_tensor(o, xx, sv, ALU.mult), a, m_free,
                           T["q", 0], T["q", 1], T["k", 2 * dr], T["k", 2 * dr + 1])
            ex_free[k_uses % 2] = [t]
            k_uses += 1
            M.append(t)
        for c in range(2):
            n = 2 * dr + c
            for tt in range(ST):
                for j in range(2):
                    hd, lo = 4 * dr + 2 * c + j, DH * j
                    b1, b2 = g.banks.take(), g.banks.take()
                    cols = slice(tt * P, (tt + 1) * P)
                    for lv in range(NL):
                        b = (b1, b2)[lv // 4]
                        if lv < NL - 1:
                            a_, b_ = Mb[lv + 1][lo:lo + DH, c, cols], Mb[lv + 1][lo:lo + DH, c, cols]
                        else:
                            a_, b_ = kk[lo:lo + DH, n, cols], q[lo:lo + DH, c, cols]
                        t = g.mm(b.ap[:, (lv % 4) * P:(lv % 4 + 1) * P], a_, b_, True, True, M, b.free, sig=(lv in (3, NL - 1)))
                        if lv == 3:
                            t1 = t
                    o = dr * NL * P
                    a1 = dve.op(lambda e, i, b=b1, o=o: e.tensor_tensor(tmp[:, 0:512], b.ap[:, :], g.c("hmask", o, 512), ALU.mult), t1, tmp_free)
                    a2 = dve.op(lambda e, i, b=b2, o=o: e.tensor_tensor(tmp[:, 512:1024], b.ap[:, :], g.c("hmask", o + 512, 512), ALU.mult), t)
                    b1.free, b2.free = [a1], [a2]
                    dst = AT[:, hd, tt * P:(tt + 1) * P]
                    a = dve.op(lambda e, i, dst=dst: e.tensor_reduce(dst, tmp.rearrange("p (l t) -> p t l", l=NL), AX.X, ALU.add), a1, a2)
                    tmp_free = [a]
                    at[hd, tt] = a
            for j in range(2):
                hd, lo = 4 * dr + 2 * c + j, DH * j
                b = g.banks.take()
                kt, qt = (0, 1) if dr == 0 else (1, 0)
                t = g.mm(b.ap[:, 0:P], Mb[0][lo:lo + DH, c, kt * P:(kt + 1) * P], Mb[0][lo:lo + DH, c, qt * P:(qt + 1) * P],
                         True, True, M, b.free, sig=True)
                a = act.op(lambda e, i, b=b, hd=hd: e.copy(AL[:, hd, :], b.ap[:, 0:P]), t)
                b.free = [a]
                at[hd, 2] = a
        m_free = [t]
    g.hgrn_read = [t, tmp_free, dve.last]
    for c in range(2):
        b = g.banks.take()
        for j in range(2):
            lo = DH * j
            f, r = 2 * c + j, 4 + 2 * c + j
            vcol = slice((2 * c + j) * DH, (2 * c + j + 1) * DH)
            needs = [at[f, n] for n in range(3)] + [at[r, n] for n in range(3)] + avt + b.free
            q0, q1 = b.ap[lo:lo + DH, 0:P], b.ap[lo:lo + DH, P:S]
            g.mm(q0, av[:, 0, vcol], AT[:, f, 0:P], True, False, needs)
            g.mm(q0, av[:, 0, vcol], AT[:, r, 0:P], False, False)
            g.mm(q0, av[:, 1, vcol], AL[:, r, :], False, True)
            g.mm(q1, av[:, 0, vcol], AL[:, f, :], True, False)
            g.mm(q1, av[:, 1, vcol], AT[:, f, P:S], False, False)
            t = g.mm(q1, av[:, 1, vcol], AT[:, r, P:S], False, True, sig=True)
        o, s2 = ex[0][:, c, :], ex[1][:, c, :]
        a = act.op(lambda e, i, b=b, o=o: e.copy(o, b.ap[:, 0:S]), t, ex_free[0])
        b.free = [a]
        a2 = act.op(lambda e, i, o=o, s2=s2: e.activation(s2, o, ACT.Square), a, ex_free[1])
        b = g.banks.take()
        t = g.mm(b.ap[:, 0:S], g.c("headones"), s2, True, True, a2, b.free, sig=True)
        dst, sc_ = ex[0][:, 2 + c, :], ex[1][:, 2 + c, :]
        r, read = inv_rms(g, b.ap[:, 0:S], dst, sc_, DH, t)
        b.free = [read]
        a = dve.op(lambda e, i, o=o, dst=dst: e.tensor_tensor(o, o, dst, ALU.mult), r, a2)
        mt[c] = dve.op(lambda e, i, o=o, c=c: e.tensor_tensor(mixed[:, c, :], o, gsil[:, c, :], ALU.mult), a, T["g", c])


def fourier(g, T, uT, V, mixed, mt):
    act, dve = g.act, g.dve
    V = V[:, :, :].rearrange("p a t -> p (a t)").rearrange("p (s c f) -> p s c f", s=ST, c=2)
    vt = []
    for c in range(2):
        for tt in range(ST):
            b = g.banks.take()
            t = g.mm(b.ap[:, 0:S], uT[:, c, tt * P:(tt + 1) * P], g.c("dft_c"), True, True, T["u", c], b.free, sig=True)
            a = act.op(lambda e, i, b=b, c=c, tt=tt: e.copy(V[:, tt, c, :], b.ap[:, 0:S]), t, g.hgrn_read)
            b.free = [a]
            vt.append(a)
    for c in range(2):
        b = g.banks.take()
        for n in range(4):
            part, tt = n // 2, n % 2
            t = g.mm(b.ap[:, 0:S], V[:, tt, c, part * P:(part + 1) * P], g.c("dft_t", (part * ST + tt) * S, S), n == 0, n == 3,
                     vt, b.free, sig=(n == 3))
        a = act.op(lambda e, i, b=b, c=c: e.copy(mixed[:, 2 + c, :], b.ap[:, 0:S]), t)
        b.free = [a]
        mt[2 + c] = a


def build(nc, ctx, dram, out):
    g = Prog(nc, ctx, dram, out)
    g.lb = ctx.enter_context(nc.sbuf_tensor("lb", [P, 16], F32))
    g.posi = ctx.enter_context(nc.sbuf_tensor("posi", [P, S], I32))
    g.base = nc.sbuf_base
    g.gate_area = lambda work, n: work[:, n * 1024:(n + 1) * 1024].rearrange("p (c t) -> p c t", c=EC)

    def fix_holds():
        for e in g.engs:
            new = []
            for it in e.items:
                if it[0] == "hold":
                    new += [("wait", t) for t in it[1]]
                else:
                    new.append(it)
            e.items[:] = new
    g.fix_holds = fix_holds
    g.t_prm, g.t_cst, g.t_tab = Tok(g.s_prm, 16), Tok(g.s_cst, 16), Tok(g.s_tab, 48)
    g.t_pool_a, g.t_pos = Tok(g.s_cst, 16), Tok(g.s_pos, 16)
    g.t_pool_a = Tok(g.s_pos, 32)
    g.t_pos = g.t_pool_a
    tx = Tok(g.s_x, 16)

    for e in g.engs:
        e.need(tx, g.t_prm, g.t_cst)
    xt = first_block(g, [tx] * KC)
    second_consts(g)
    g.dve.need(Tok(g.s_mask, 16))
    g.meet(clear=True)
    g.open(0, DEPTH2, counted=False)
    second_layer(g)
    g.meet(clear=True)
    g.close()
    x, h = (t[:, :].rearrange("p (k t) -> p k t", k=KC) for t in (g.x, g.h))
    g.top = g.base
    sq = g.area("sqf", KC * S)[:, :].rearrange("p (c t) -> p c t", c=KC)
    rs, scr = g.area("rsf", S)[:, :], g.area("scrf", S)[:, :]
    final = rms_norm(g, x, [None] * KC, g.p("gf2"), None, h, sq, rs, scr)
    assert g.tile == N_TILES, (g.tile, N_TILES)

    a0, a1 = CST["pool_a"]
    assert a1 - a0 == 2 * NL * P
    with nc.Block() as block:
        @block.sync
        def _(sp):
            sp.dma_start(g.x[:, :], dram["x"]).then_inc(g.s_x, 16)
            sp.dma_start(g.prm[:, :], dram["prm"]).then_inc(g.s_prm, 16)
            for s in range(R):
                sp.dma_start(g.ring[s][:, :], dram["weights"][s]).then_inc(g.s_slot[s], 16)
            with sp.Fori(1, N_TILES // R) as i:
                for s in range(R):
                    sp.wait_ge(g.s_freed, (i - 1) * R + s + 1)
                    sp.dma_start(g.ring[s][:, :], dram["weights"][bass.ds(i * R + s, 1)].rearrange("a p f -> (a p) f")).then_inc(g.s_slot[s], 16)

        @block.scalar
        def _(e):
            e.dma_start(g.cst[:, :], dram["cst"][:, 0:a0]).then_inc(g.s_cst, 16)
            e.dma_start(g.tab[0:BUCKETS, :], dram["tab"][0:BUCKETS, :]).then_inc(g.s_tab, 16)
            e.dma_start(g.tab_neg[0:HEADS, :], dram["tab"][BUCKETS:BUCKETS + 1, :].to_broadcast([HEADS, NB_ROW])).then_inc(g.s_tab, 16)
            e.dma_start(g.rb[0:BUCKETS, :], dram["rel"]).then_inc(g.s_tab, 16)
            e.dma_start(g.pool_a[:, :], dram["cst"][:, a0:a1]).then_inc(g.s_pos, 16)
            e.dma_start(g.posi[:, :], dram["pos"].to_broadcast([P, S])).then_inc(g.s_pos, 16)
            g.act.emit(e)
            for n in range(2):
                t = final[4 * n + 3]
                e.wait_ge(t.sem, t.n)
                cols = slice(n * 4 * S, (n + 1) * 4 * S)
                e.dma_start(out[:, cols], g.h[:, cols]).then_inc(g.s_out, 16)
            e.wait_ge(g.s_out, 32)

        @block.tensor
        def _(e):
            g.pe.emit(e)

        @block.vector
        def _(e):
            g.dve.emit(e)

        @block.gpsimd
        def _(e):
            e.wait_ge(g.t_row.sem, g.t_row.n)
            e.dma_start(dram["row"], g.row[0:HEADS, :]).then_inc(g.s_row, 16)
            e.wait_ge(g.s_row, 16)
            for qt in range(ST):
                nk = (qt + 1) * P
                src = bass.AP(dram["row"].tensor, 0, [[1, P], [NB_ROW, HEADS], [1, nk]])
                o = 0 if qt == 0 else HEADS * P
                e.dma_start(g.bias[:, o:o + HEADS * nk].rearrange("p (h k) -> p h k", h=HEADS), src).then_inc(g.s_bias, 16)
            e.wait_ge(g.s_bias, 32)
            e.wait_ge(g.t_pooled.sem, g.t_pooled.n)
            e.dma_start(g.pool_a[:, :], dram["cst"][:, a1:]).then_inc(g.s_mask, 16)
            g.pool.emit(e)


def kernel(**inputs):
    from contextlib import ExitStack
    import concourse.bacc as bacc
    from concourse.bass_utils import run_bass_kernel_spmd

    a = {k: np.asarray(v) for k, v in inputs.items()}
    vec = lambda v: v.reshape(-1, P).T

    def cols(w, width):
        k, n = w.shape
        return w.reshape(k // P, P, n // width, width).transpose(2, 1, 0, 3).reshape(-1, P, (k // P) * width)

    w_in = a["w_in"][0]
    tiles = [cols(a["w_ada"][0][:, :2048], 256), cols(w_in[:, :1024], 256), cols(w_in[:, 1024:2048], 256),
             cols(w_in[:, 2048:], 256), cols(a["w_ada"][0][:, 2048:], 256),
             cols(a["w_branch_attn"][0], 512), cols(a["w_branch_pool"][0], 512), cols(a["w_out"][0], 256)]
    n0 = sum(t.shape[0] for t in tiles)
    wg = a["w_expert_gate"][0].reshape(NE, KC, P, 2, 256).transpose(0, 3, 2, 1, 4).reshape(NE, 2, 1, P, TILE)
    wu = a["w_expert_up"][0].reshape(NE, KC, P, 2, 256).transpose(0, 3, 2, 1, 4).reshape(NE, 2, 1, P, TILE)
    wd = a["w_expert_down"][0].reshape(NE, EC, P, 2, 512).transpose(0, 3, 2, 1, 4).reshape(NE, 2, P, TILE)
    ex = np.concatenate([np.concatenate([wg, wu], 2).reshape(NE, 4, P, TILE), wd], 1).reshape(-1, P, TILE)
    tiles.append(ex)
    for l in range(DEPTH2):
        w = a["w_in_2"][l]
        W = 256
        part = lambda lo, n: w[:, lo:lo + n]
        order = [part(0, W), part(4 * W, W), part(2 * W, W), part(3 * W, W), part(5 * W, W), part(6 * W, 1024),
                 part(W, W), part(6 * W + 1024, 512)]
        tiles += [cols(o, 256) for o in order]
        tiles += [cols(a["w_out_2"][l], 256), cols(a["w_up_2"][l], 256)]
        wdn = a["w_down_2"][l].reshape(2, 16, P, KC, P).transpose(3, 0, 2, 1, 4).reshape(-1, P, TILE)
        tiles.append(wdn)
    weights = np.concatenate([t.reshape(-1, P, TILE) for t in tiles])
    assert weights.shape[0] == N_TILES, weights.shape

    prm = np.zeros((P, N_PRM), np.float32)

    def put(name, v):
        lo, hi = PRM[name]
        prm[:, lo:hi] = v.reshape(P, hi - lo)

    put("b_ada", vec(a["b_ada"][0]))
    put("g1", vec(a["norm1_g"][0]))
    put("b_gate", vec(a["b_gate"][0]))
    put("pool_scale", vec(a["pool_scale"][0]))
    put("g2", vec(a["norm2_g"][0]))
    put("gf", vec(a["norm_f_g"]))
    put("c", vec(a["c"][0]))
    put("gf2", vec(a["final_norm_w_2"]))
    put("layer", np.concatenate([v for l in range(DEPTH2) for v in (vec(a["attn_norm_w_2"][l]), vec(a["mlp_norm_w_2"][l]))], 1))
    put("lb_raw", vec(a["hgrn_lower_bounds_2"].reshape(-1)))
    put("b_router", np.broadcast_to(np.concatenate([a["b_router_group"][0], a["b_router_expert"][0]]), (P, 36)))
    wr = np.concatenate([a["w_router_group"][0], a["w_router_expert"][0]], 1)
    put("w_router", wr.reshape(KC, P, 36).transpose(1, 0, 2))
    put("pool_w", a["pool_w"][0].transpose(1, 0, 2))
    x = np.ascontiguousarray(a["x"][0].T.reshape(KC, P, S).transpose(1, 0, 2)).reshape(P, KC * S)
    arrays = {"weights": weights, "prm": prm, "x": x, "cst": constants(), "tab": bias_table(),
              "rel": np.ascontiguousarray(a["rel_bias"]), "pos": np.ascontiguousarray(a["positions_2"]).astype(np.int32).reshape(1, S)}

    nc = bacc.Bacc("TRN2", target_bir_lowering=False, num_devices=1)
    dram = {k: nc.dram_tensor("in_" + k, v.shape, mybir.dt.from_np(v.dtype), kind="ExternalInput").ap() for k, v in arrays.items()}
    dram["row"] = nc.dram_tensor("bias_rows", (HEADS, NB_ROW), F32, kind="Internal").ap()
    out = nc.dram_tensor("out", (P, KC * S), F32, kind="ExternalOutput").ap()
    with ExitStack() as ctx:
        build(nc, ctx, dram, out)
    r = run_bass_kernel_spmd(nc, [{"in_" + k: v for k, v in arrays.items()}], core_ids=[0])
    y = r.results[0]["out"].reshape(P, KC, S)
    return y.transpose(2, 1, 0).reshape(1, S, D)
```

```python
import concourse.bass as bass
import concourse.mybir as mybir
import numpy as np
from concourse.alu_op_type import AluOpType as ALU

F32 = mybir.dt.float32
F32R = mybir.dt.float32r
I32 = mybir.dt.int32
ACT = mybir.ActivationFunctionType
AX = mybir.AxisListType

P = 128
D = 1024
S = 256
KC = D // P
ST = S // P
HEADS, DH = 8, 64
EPS = 1e-6
NEG = -1e30
WINDOWS = (2, 4, 8, 16)
BUCKETS = 32
GROUPS, PER_GROUP = 4, 8
NE = GROUPS * PER_GROUP
SLOTS = 64
CAP = SLOTS
DE = 512
EC = DE // P
DEPTH2 = 2
LEVELS = (64, 32, 16, 8, 4, 2, 1)
NL = len(LEVELS) + 1
DFF = 4096

TILE = 2048
R = 12
AHEAD = 2
T_ADA, T_IN, T_BRANCH, T_OUT = 24, 16, 4, 4
T_EXPERT = 6
T_LAYER = 12 + 4 + 16 + 16
N_TILES = T_ADA + T_IN + T_BRANCH + T_OUT + NE * T_EXPERT + DEPTH2 * T_LAYER

R_EXPERTS = (T_ADA + T_IN + T_BRANCH + T_OUT) // R
R_LAYERS = R_EXPERTS + NE * T_EXPERT // R
assert NE * T_EXPERT % R == 0 and T_LAYER % R == 0 and 2 * T_EXPERT == R

PRM = {}
_o = 0
for _n, _w in (("b_ada", 48), ("g1", 8), ("b_gate", 16), ("pool_scale", 4), ("g2", 8), ("gf", 8),
               ("c", 8), ("gf2", 8), ("layer", DEPTH2 * 16), ("lb_raw", DEPTH2 * 4), ("b_router", 36),
               ("w_router", 8 * 36), ("pool_w", 4 * 128)):
    PRM[_n] = (_o, _o + _w)
    _o += _w
N_PRM = _o

CST = {}
_o = 0
for _n, _w in (("ident", P), ("ones", P), ("headones", P), ("perm", P), ("invf", 1),
               ("first4", 4), ("first32", NE), ("lnmask", ST * S), ("dft_c", 2 * P),
               ("dft_t", 2 * ST * S), ("pool_a", 4 * ST * S), ("hmask", 2 * NL * P)):
    CST[_n] = (_o, _o + _w)
    _o += _w
N_CST = _o
NB_ROW = 3 * P


def constants():
    c = np.zeros((P, N_CST), np.float32)
    pos, row = np.arange(S), np.arange(P)

    def put(name, a):
        lo, hi = CST[name]
        c[:, lo:hi] = np.asarray(a, np.float64).reshape(P, hi - lo).astype(np.float32)

    put("ident", np.eye(P))
    put("ones", np.ones((P, P)))
    put("headones", (row[:, None] // DH == row[None] // DH))
    perm = np.zeros((P, P))
    for m in row:
        if m % DH < DH // 2:
            perm[m + DH // 2, m] = -1.0
        else:
            perm[m - DH // 2, m] = 1.0
    put("perm", perm)
    inv = np.float32(10000.0) ** (-np.arange(0, DH, 2, dtype=np.float32) / np.float32(DH))
    put("invf", inv[row % (DH // 2)])
    put("first4", np.broadcast_to(GROUPS - np.arange(GROUPS), (P, GROUPS)))
    put("first32", np.broadcast_to(NE - np.arange(NE), (P, NE)))
    dist = np.abs(pos[:, None] - pos[None])
    count = (dist <= 64) * 1 + (dist % 4 == 0) * 1 + (dist % 16 == 0) * 1
    ln = np.where(count > 0, np.log(np.maximum(count, 1)), NEG)
    put("lnmask", ln.reshape(ST, P, S).transpose(1, 0, 2))
    k = np.arange(DH)
    ang = 2 * np.pi * ((k[:, None] * k[None]) % DH) / DH
    blk = np.kron(np.eye(2), np.cos(ang)), np.kron(np.eye(2), np.sin(ang))
    put("dft_c", np.stack(blk, 1) / np.sqrt(DH))
    ang = 2 * np.pi * ((pos[:, None] * pos[None]) % S) / S
    dt = np.stack([np.cos(ang), -np.sin(ang)]) / np.sqrt(S)
    put("dft_t", dt.reshape(2, ST, P, S).transpose(2, 0, 1, 3))
    m = np.zeros((P, 2, NL, P))
    for n, h in enumerate(LEVELS):
        same = row[:, None] // (2 * h) == row[None] // (2 * h)
        left, right = row // h % 2 == 0, row // h % 2 == 1
        m[:, 0, n] = same & left[:, None] & right[None]
        m[:, 1, n] = same & right[:, None] & left[None]
    m[:, :, NL - 1] = np.eye(P)[:, None]
    put("hmask", m)
    a = np.zeros((4, S, S))
    for g, w in enumerate(WINDOWS):
        for t in pos:
            lo = max(t + 1 - w, 0)
            a[g, lo:t + 1, t] = 1.0 / (t + 1 - lo)
            a[g, t, t] -= 1.0
    put("pool_a", a.reshape(4, ST, P, S).transpose(2, 0, 1, 3))
    return c


def slot_constants():
    row = np.arange(P)
    tri = (row[:, None] < row[None]).astype(np.float32)
    slots = np.arange(2 * SLOTS, dtype=np.float32) % SLOTS
    fold = (row[:, None] % SLOTS == np.arange(SLOTS)[None]).astype(np.float32)
    return np.concatenate([tri, np.broadcast_to(slots, (P, 2 * SLOTS)), fold], 1)


def bias_table():
    m = np.arange(NB_ROW)
    n = np.maximum(m - (P - 1), 0)
    nf = np.maximum(n, 1).astype(np.float32)
    big = 16 + (np.log(nf / np.float32(16)) / np.float32(np.log(8.0)) * np.float32(16)).astype(np.int32)
    b = np.where(n < 16, n, np.minimum(big, BUCKETS - 1))
    t = np.zeros((BUCKETS + 1, NB_ROW), np.float32)
    past = m >= P - 1
    t[b[past], m[past]] = 1.0
    t[BUCKETS, ~past] = NEG
    return t


class Tok:

    def __init__(self, sem, n, loop=None, lag=0):
        self.sem, self.n, self.loop, self.lag = sem, n, loop, lag

    def before(self):
        return Tok(self.sem, self.n, self.loop, 1)


class Loop:
    def __init__(self, start, count, counted):
        self.start, self.count, self.counted, self.per = start, count, counted, {}


class Eng:

    def __init__(self, prog, name, sem):
        self.prog, self.name, self.sem, self.n = prog, name, sem, 0
        self.items = []
        self.known = {}
        self.last = None

    def need(self, *toks):
        for t in toks:
            if t is None:
                continue
            if isinstance(t, (list, tuple)):
                self.need(*t)
                continue
            key = (id(t.sem), t.lag, t.loop is not None)
            if self.known.get(key, 0) >= t.n:
                continue
            self.known[key] = t.n
            self.items.append(("wait", t))

    def op(self, fn, *needs, sig=True):
        self.need(*needs)
        if not sig:
            self.items.append(("op", fn, None))
            return None
        self.n += 1
        self.items.append(("op", fn, self.sem))
        self.last = Tok(self.sem, self.n, self.prog.loop)
        return self.last

    def raise_(self, sem, n=1):
        self.items.append(("inc", sem, n))

    def emit(self, e):
        stack = [(e, 0, None)]
        i = 0
        ctxs = []
        loop = None
        for it in self.items:
            kind = it[0]
            if kind == "wait":
                t = it[1]
                v = t.n
                if t.loop is not None and t.loop is loop:
                    per = t.loop.per.get(id(t.sem), 0)
                    if per:
                        v = t.n + (i - t.loop.start - t.lag) * per
                e.wait_ge(t.sem, v)
            elif kind == "op":
                ins = it[1](e, i)
                if it[2] is not None:
                    ins.then_inc(it[2], 1)
            elif kind == "inc":
                e.sem_inc(it[1], it[2])
            elif kind == "clear":
                e.sem_clear(it[1])
            elif kind == "if":
                most = e.value_load(it[1])
                ctx = e.If(most > CAP)
                ctx.__enter__()
                ctxs.append(ctx)
            elif kind == "loop":
                loop = it[1]
                ctx = e.Fori(loop.start, loop.start + loop.count)
                i = ctx.__enter__()
                ctxs.append(ctx)
            elif kind == "end":
                ctxs.pop().__exit__(None, None, None)
                i, loop = 0, None


class Rot:

    def __init__(self, aps):
        self.slots = [Slot(a) for a in aps]
        self.k = 0

    def take(self):
        s = self.slots[self.k % len(self.slots)]
        self.k += 1
        return s


class Slot:
    def __init__(self, ap):
        self.ap, self.free = ap, []


class Prog:
    def __init__(self, nc, ctx, dram, out):
        self.nc, self.ctx, self.dram, self.out = nc, ctx, dram, out
        self.loop = None
        sem = lambda n: ctx.enter_context(nc.semaphore(n))
        self.pe, self.act, self.dve, self.pool = (Eng(self, n, sem("done_" + n)) for n in ("pe", "act", "dve", "pool"))
        self.engs = [self.pe, self.act, self.dve, self.pool]
        self.s_slot = [sem(f"slot_filled_{i}") for i in range(R)]
        self.s_freed = sem("slots_freed")
        self.s_x, self.s_prm, self.s_cst, self.s_tab, self.s_pos = (sem(n) for n in ("x_in", "prm_in", "cst_in", "tab_in", "pos_in"))
        self.s_row, self.s_bias, self.s_out, self.s_mask = sem("bias_row_out"), sem("bias_in"), sem("result_out"), sem("mask_in")
        self.s_over = [sem(f"over_filled_{i}") for i in range(R)]
        self.s_over_freed, self.s_flag, self.s_slots = sem("over_freed"), sem("most_known"), sem("slot_cst_in")
        self.s_arrive = sem("engines_arrived")
        self.s_go = {e: sem("go_" + e.name) for e in self.engs}
        self.tile = 0
        self.to_free = 0
        fix = lambda n, cols, dt=F32: ctx.enter_context(nc.sbuf_tensor(n, [P, cols], dt))
        self.ring = [fix(f"ring{i}", TILE) for i in range(R)]
        self.x = fix("x", KC * S)
        self.h = fix("h", KC * S)
        self.prm = fix("prm", N_PRM)
        self.cst = fix("cst", CST["pool_a"][0])
        self.pool_a = fix("pool_a", 2 * NL * P)
        self.rope = fix("rope", 2 * S)
        self.small = fix("small", 256)
        self.small_used = 0
        self.cur = fix("cur", 24)
        self.base = nc.sbuf_base
        self.top = self.base
        self.bank = [ctx.enter_context(nc.psum_tensor(f"bank{i}", [P, 512], F32)) for i in range(8)]
        self.banks = Rot([b[:, :] for b in self.bank])

    def area(self, name, cols, dt=F32):
        off = (self.top + 31) // 32 * 32
        t = self.nc.alloc_sbuf_tensor_at(name, [P, cols], dt, offset=off)
        self.top = off + cols * 4
        assert self.top <= self.nc.sbuf_usable_end, (name, self.top)
        return t

    def at(self, name, off, cols, dt=F32):
        return self.nc.alloc_sbuf_tensor_at(name, [P, cols], dt, offset=off), off + cols * 4

    def col(self, n=1):
        a = self.small_used
        self.small_used += n
        assert self.small_used <= 256
        return self.small[:, a:a + n]

    def p(self, name, a=0, n=None):
        lo, hi = PRM[name]
        return self.prm[:, lo + a:(lo + a + n) if n is not None else hi]

    def c(self, name, a=0, n=None):
        lo, hi = CST[name]
        if name == "hmask":
            return self.pool_a[:, a:a + n]
        return self.cst[:, lo + a:(lo + a + n) if n is not None else hi]

    def next_tile(self):
        slot, fill = self.tile % R, self.tile // R + 1
        self.tile += 1
        return self.ring[slot], Tok(self.s_slot[slot], 16 * fill, self.loop)

    def done_tile(self):
        self.to_free += 1

    def tile_at(self, k):
        return self.ring[k], Tok(self.s_over[k], 16, self.loop)

    def only_if_over(self, path):
        kept = [(e.n, e.last) for e in self.engs]
        for e in self.engs:
            e.items.append(("if", self.most[0:1, 0:1]))
            e.known = {}
        path()
        for e, (n, last) in zip(self.engs, kept):
            e.items.append(("end",))
            e.n, e.last, e.known = n, last, {}
        self.meet(clear=True)

    def mm(self, out, lhsT, rhs, start, stop, *needs, sig=False, skip=False, transpose=False):
        pe = self.pe
        if transpose:
            fn = lambda e, i: e.transpose(out, lhsT, rhs)
        else:
            fn = lambda e, i: e.matmul(out, lhsT, rhs, start=start, stop=stop, skip_group_check=skip)
        pe.need(*needs)
        if not sig and self.to_free:
            self.to_free -= 1
            pe.items.append(("op", fn, self.s_freed))
            return None
        return pe.op(fn, sig=sig)

    def flush_tiles(self):
        if self.to_free:
            self.pe.need(self.pe.last)
            self.pe.raise_(self.s_freed, self.to_free)
            self.to_free = 0

    def meet(self, clear):
        lead = self.dve
        for e in self.engs:
            e.need(e.last)
            if e is not lead:
                e.raise_(self.s_arrive)
        lead.items.append(("wait", Tok(self.s_arrive, 3)))
        if clear:
            for e in self.engs:
                lead.items.append(("clear", e.sem))
        lead.items.append(("clear", self.s_arrive))
        for e in self.engs:
            if e is not lead:
                lead.raise_(self.s_go[e])
                e.items.append(("wait", Tok(self.s_go[e], 1)))
                e.items.append(("clear", self.s_go[e]))
            if clear:
                e.n, e.last = 0, None
            e.known = {}
        for s in self.banks.slots:
            s.free = []

    def open(self, start, count, counted):
        self.loop = Loop(start, count, counted)
        self.loop0 = {e: e.n for e in self.engs}, self.tile
        for e in self.engs:
            e.items.append(("loop", self.loop))
            e.known = {}

    def close(self):
        lp = self.loop
        n0, t0 = self.loop0
        for e in self.engs:
            if lp.counted:
                per = e.n - n0[e]
                lp.per[id(e.sem)] = per
                e.n = n0[e] + per * lp.count
                if e.last is not None:
                    e.last = Tok(e.sem, e.n)
            e.items.append(("end",))
            e.known = {}
        tiles = self.tile - t0
        assert tiles % R == 0
        for s in self.s_slot:
            lp.per[id(s)] = 16 * tiles // R
        for s in self.s_over:
            lp.per[id(s)] = 16
        self.tile = t0 + tiles * lp.count
        self.loop = None


def nothing():
    pass


def linear(g, acts, toks, n_out, kc, width, evac, after=(), before=nothing, behind=nothing):
    per = width // P
    for oc in range(n_out):
        if oc % per == 0:
            before()
            w, filled = g.next_tile()
        b = g.banks.take()
        j = oc % per
        for k in range(kc):
            t = g.mm(b.ap[:, 0:S], w[:, k * width + j * P:k * width + (j + 1) * P], acts[:, k, :],
                     k == 0, k == kc - 1, filled, toks[k], b.free if k == 0 else None, after, sig=(k == kc - 1))
        if j == per - 1:
            g.done_tile()
        b.free = [evac(oc, b.ap[:, 0:S], t)]
        if j == per - 1:
            behind()


def linear_tokens(g, acts, toks, n_cols, evac, before=nothing, behind=nothing):
    for j in range(n_cols // 256):
        before()
        w, filled = g.next_tile()
        for tt in range(ST):
            b = g.banks.take()
            for k in range(KC):
                t = g.mm(b.ap[:, 0:256], acts[:, k, tt * P:(tt + 1) * P], w[:, k * 256:(k + 1) * 256],
                         k == 0, k == KC - 1, filled, toks[k], b.free if k == 0 else None, sig=(k == KC - 1))
            b.free = [evac(j, tt, b.ap[:, 0:256], t)]
        g.done_tile()
        behind()


def inv_rms(g, psum, out, scratch, n, t, free=()):
    a = g.dve.op(lambda e, i: e.tensor_scalar(scratch, psum, 1.0 / n, EPS, ALU.mult, ALU.add), t, *free)
    b = g.dve.op(lambda e, i: e.reciprocal(scratch, scratch), a)
    return g.act.op(lambda e, i: e.activation(out, scratch, ACT.Sqrt), b), a


def rms(g, x, xt, sq, rs, scratch, after=()):
    b = g.banks.take()
    for k in range(KC):
        s = g.act.op(lambda e, i, k=k: e.activation(sq[:, k, :], x[:, k, :], ACT.Square), xt[k], *after)
        t = g.mm(b.ap[:, 0:S], g.c("ones"), sq[:, k, :], k == 0, k == KC - 1, s, b.free if k == 0 else None,
                 sig=(k == KC - 1))
    r, read = inv_rms(g, b.ap[:, 0:S], rs, scratch, D, t)
    b.free = [read]
    return r


def rms_apply(g, x, xt, scale, shift, h, rs, r, after=()):
    toks = []
    for k in range(KC):
        a = g.dve.op(lambda e, i, k=k: e.scalar_tensor_tensor(out=h[:, k, :], in0=x[:, k, :], scalar=scale[:, k:k + 1],
                                                              in1=rs, op0=ALU.mult, op1=ALU.mult), r, xt[k], *after)
        if shift is not None:
            a = g.act.op(lambda e, i, k=k: e.activation(h[:, k, :], h[:, k, :], ACT.Identity, bias=shift[:, k:k + 1]), a)
        toks.append(a)
    return toks


def rms_norm(g, x, xt, scale, shift, h, sq, rs, scratch, after=()):
    return rms_apply(g, x, xt, scale, shift, h, rs, rms(g, x, xt, sq, rs, scratch, after), after)


def attention(g, q, k, v, qk_toks, v_toks, add, add_tok, causal, out, pbuf, ptbuf, out_toks):
    state = {}

    def scores(c):
        for j in range(2):
            for qt in range(ST):
                hd, lo = 2 * c + j, DH * j
                nk = (qt + 1) * P if causal else S
                b, pb = g.banks.take(), pbuf.take()
                t = g.mm(b.ap[:, 0:nk], q[lo:lo + DH, c, qt * P:(qt + 1) * P], k[lo:lo + DH, c, 0:nk],
                         True, True, qk_toks[c], b.free, sig=True)
                m, s = g.col(), g.col()
                pr = pb.ap[:, 0:nk]
                a = g.dve.op(lambda e, i, pr=pr, b=b, nk=nk, hd=hd, qt=qt: e.scalar_tensor_tensor(
                    out=pr, in0=b.ap[:, 0:nk], scalar=DH ** -0.5, in1=add(hd, qt), op0=ALU.mult, op1=ALU.add),
                    t, add_tok, pb.free)
                b.free = [a]
                a = g.dve.op(lambda e, i, m=m, pr=pr: e.tensor_reduce(m, pr, AX.X, ALU.max, negate=True), a)
                a = g.act.op(lambda e, i, m=m, s=s, pr=pr: e.activation(pr, pr, ACT.Exp, bias=m, accum_out=s), a)
                a = g.dve.op(lambda e, i, s=s: e.reciprocal(s, s), a)
                a = g.dve.op(lambda e, i, s=s, pr=pr: e.tensor_scalar(pr, pr, s, None, ALU.mult), a)
                state[c, j, qt] = pb, a

    def turn(c):
        for j in range(2):
            b, pt = g.banks.take(), ptbuf.take()
            pieces = [(kt, qt) for kt in range(ST) for qt in range(ST) if not (causal and kt > qt)]
            for n, (kt, qt) in enumerate(pieces):
                pb, a = state[c, j, qt]
                t = g.mm(b.ap[:, n * P:(n + 1) * P], pb.ap[:, kt * P:(kt + 1) * P], g.c("ident"), True, True,
                         a, b.free, sig=True, transpose=True)
            for qt in range(ST):
                state[c, j, qt][0].free = [t]
            w = len(pieces) * P
            a = g.act.op(lambda e, i, pt=pt, b=b, w=w: e.copy(pt.ap[:, 0:w], b.ap[:, 0:w]), t, pt.free)
            b.free = [a]
            state[c, j] = pt, a

    def mix(c):
        b = g.banks.take()
        for j in range(2):
            pt, a = state[c, j]
            hd, lo = 2 * c + j, DH * j
            w = S if not causal else P
            g.mm(b.ap[lo:lo + DH, 0:S], v[:, 0, hd * DH:(hd + 1) * DH], pt.ap[:, 0:S], True, False,
                 a, v_toks, b.free)
            t = g.mm(b.ap[lo:lo + DH, S - w:S], v[:, 1, hd * DH:(hd + 1) * DH], pt.ap[:, S:S + w], False, True, sig=True)
            pt.free = [t]
        a = g.act.op(lambda e, i, b=b: e.copy(out[:, c, :], b.ap[:, 0:S]), t)
        b.free = [a]
        out_toks.append(a)

    n = HEADS // 2
    for c in range(n + 2):
        if c < n:
            scores(c)
        if 1 <= c <= n:
            turn(c - 1)
        if c >= 2:
            mix(c - 2)
        yield


def first_block(g, xt):
    pe, act, dve, pool = g.pe, g.act, g.dve, g.pool
    g.top = g.base
    x, h = (t[:, :].rearrange("p (k t) -> p k t", k=KC) for t in (g.x, g.h))
    prm, cst = g.t_prm, g.t_cst
    pool_a = g.pool_a
    bias = g.area("bias", HEADS * 384)
    g.bias = bias
    q = g.area("q1", 4 * S)
    k_off = g.top
    k, u = (g.area(n, 4 * S) for n in ("k1", "u1"))
    v_off = g.top
    v = g.area("v1", 4 * S)
    q3, k3 = (t[:, :].rearrange("p (c t) -> p c t", c=4) for t in (q, k))
    v3, u3 = (t[:, :].rearrange("p (s f) -> p s f", s=ST) for t in (v, u))
    gate = g.area("gate", 16 * S)
    gate3 = gate[:, :].rearrange("p (c t) -> p c t", c=16)
    att = g.area("att1", 4 * S)[:, :].rearrange("p (c t) -> p c t", c=4)
    pol = q3
    pbuf = Rot([g.area(f"p1_{i}", S)[:, :] for i in range(8)])
    ptbuf = Rot([g.area(f"pt1_{i}", 2 * S)[:, :] for i in range(4)])
    rs, scr = g.area("rs1", S)[:, :], g.area("scr1", S)[:, :]
    g.mod_off = g.top
    mod = g.area("mod", 48)
    mod1 = g.area("mod1", 48)
    cact, sc1, sc2 = (g.area(n, KC) for n in ("cact", "sc1", "sc2"))
    g.rb = g.area("rb", 8)
    a_tmp = g.area("a_tmp", 2 * EC * SLOTS)
    g.tab, g.row, g.tab_neg = (gate[:, 2048 + n * NB_ROW:2048 + (n + 1) * NB_ROW] for n in range(3))

    ca = act.op(lambda e, i: e.activation(cact[:, :], g.p("c"), ACT.Silu), prm)

    b = g.banks.take()
    t = g.mm(b.ap[0:HEADS, 0:NB_ROW], g.rb[0:BUCKETS, 0:HEADS], g.tab[0:BUCKETS, :], True, True, g.t_tab, sig=True)
    a = dve.op(lambda e, i, b=b: e.tensor_tensor(g.row[0:HEADS, :], b.ap[0:HEADS, 0:NB_ROW], g.tab_neg[0:HEADS, :], ALU.add), t, g.t_tab)
    b.free = [a]
    g.t_row = a
    bias_tok = Tok(g.s_bias, 32)

    def add(hd, qt):
        o = hd * P if qt == 0 else HEADS * P + hd * S
        nk = (qt + 1) * P
        return bias[:, o:o + nk][:, ::-1]

    acc = [g.area(f"ada_acc{n}", 256) for n in range(2)]
    acc_read, pend, ada_n = [None, None], [], [0]

    def ada_mul():
        w, filled = g.next_tile()
        n = ada_n[0]
        ada_n[0] += 1
        o = acc[n % 2][:, :]
        a = dve.op(lambda e, i: e.tensor_scalar(o, w[:, 0:256], cact[:, 0:1], None, ALU.mult), filled, ca, acc_read[n % 2])
        for kk in range(1, KC):
            a = dve.op(lambda e, i, kk=kk: e.scalar_tensor_tensor(out=o, in0=w[:, kk * 256:(kk + 1) * 256], scalar=cact[:, kk:kk + 1],
                                                                 in1=o, op0=ALU.mult, op1=ALU.add), a)
        pend.append((n, a))

    def ada_sum(ps, free):
        n, a = pend.pop()
        for j in range(2):
            t = g.mm(ps[:, j:j + 1], acc[n % 2][:, j * P:(j + 1) * P], g.c("ones", 0, 1), True, True, a, free, sig=(j == 1))
        acc_read[n % 2] = t
        g.done_tile()
        return t, n

    def ada_bias(ps, c0, m, t):
        return dve.op(lambda e, i: e.tensor_tensor(mod[:, c0:c0 + m], ps, g.p("b_ada", c0, m), ALU.add), t)

    def ada_step():
        b = g.banks.take()
        t, n = ada_sum(b.ap, b.free)
        b.free = [ada_bias(b.ap[:, 0:2], 2 * n, 2, t)]

    sq = gate[:, 0:KC * S].rearrange("p (k t) -> p k t", k=KC)
    rs_t = rms(g, x, xt, sq, rs, scr)
    b = g.banks.take()
    for n in range(8):
        ada_mul()
        t, _ = ada_sum(b.ap[:, 2 * n:2 * n + 2], b.free)
    a = ada_bias(b.ap[:, 0:16], 0, 16, t)
    b.free = [a]
    a = dve.op(lambda e, i: e.tensor_scalar(mod1[:, 8:16], mod[:, 8:16], 1.0, None, ALU.add), a)
    a = dve.op(lambda e, i: e.tensor_tensor(sc1[:, :], mod1[:, 8:16], g.p("g1"), ALU.mult), a)
    ht = rms_apply(g, x, xt, sc1[:, :], mod[:, 0:8], h, rs, rs_t, after=(a,))

    second_consts(g, [b.ap for b in pbuf.slots[0:5]])
    for b in pbuf.slots[0:5]:
        b.free = [act.last, dve.last]

    qk = []
    def ev_qk(oc, ps, t):
        dst = (q3 if oc < 4 else k3)[:, oc % 4, :]
        a = act.op(lambda e, i: e.copy(dst, ps), t)
        qk.append(a)
        return a
    linear(g, h, ht, 8, KC, 256, ev_qk, before=ada_mul, behind=ada_step)
    vt, ut = [], []
    def ev_vu(j, tt, ps, t):
        dst = (v3 if j < 2 else u3)[:, tt, (j % 2) * 256:(j % 2 + 1) * 256]
        a = dve.op(lambda e, i: e.tensor_copy(dst, ps), t)
        (vt if j < 2 else ut).append(a)
        return a
    linear_tokens(g, h, ht, 1024, ev_vu, before=ada_mul, behind=ada_step)
    att_t = []
    steps = attention(g, q3, k3, v3, [[qk[c], qk[4 + c]] for c in range(4)], vt, add, bias_tok, True, att, pbuf, ptbuf, att_t)

    gt = []
    act.need(Tok(g.s_row, 16))
    def ev_gate(oc, ps, t):
        a = act.op(lambda e, i: e.activation(gate3[:, oc, :], ps, ACT.Sigmoid, bias=g.p("b_gate", oc, 1)), t)
        gt.append(a)
        return a
    def behind_gate():
        ada_step()
        next(steps, None)
    next(steps, None)
    linear(g, h, ht, 16, KC, 256, ev_gate, before=ada_mul, behind=behind_gate)
    for _ in steps:
        pass
    ada_t = dve.op(lambda e, i: e.tensor_scalar(mod1[:, 16:48], mod[:, 16:48], 1.0, None, ALU.add), dve.last)

    pol_t = []
    for gr in range(4):
        b = g.banks.take()
        for tt in range(ST):
            o = (gr * ST + tt) * S
            t = g.mm(b.ap[:, 0:S], u3[:, tt, gr * P:(gr + 1) * P], pool_a[:, o:o + S], tt == 0, tt == ST - 1,
                     ut, g.t_pool_a, b.free, sig=(tt == ST - 1))
        dif = pbuf.take()
        a = act.op(lambda e, i, b=b, dif=dif: e.copy(dif.ap, b.ap[:, 0:S]), t, dif.free)
        b.free = [a]
        b2 = g.banks.take()
        t = g.mm(b2.ap[:, 0:S], g.p("pool_w", gr * P, P), dif.ap, True, True, a, b2.free, sig=True)
        dif.free = [t]
        a = act.op(lambda e, i, b=b2, gr=gr: e.mul(pol[:, gr, :], b.ap[:, 0:S], g.p("pool_scale", gr, 1)), t, att_t[-1])
        b2.free = [a]
        pol_t.append(a)
    g.t_pooled = t

    g.t_k_free = g.t_pooled

    mixed = h
    h_read = pe.last
    mt = [None] * KC
    def ev_attn(oc, ps, t):
        mt[oc] = dve.op(lambda e, i: e.tensor_tensor(mixed[:, oc, :], gate3[:, oc, :], ps, ALU.mult), t, gt, h_read)
        return mt[oc]
    linear(g, att, att_t, KC, 4, 512, ev_attn)
    def ev_pool(oc, ps, t):
        a = dve.op(lambda e, i: e.tensor_tensor(gate3[:, 8 + oc, :], gate3[:, 8 + oc, :], ps, ALU.mult), t)
        mt[oc] = dve.op(lambda e, i: e.tensor_tensor(mixed[:, oc, :], mixed[:, oc, :], gate3[:, 8 + oc, :], ALU.add), a)
        return a
    linear(g, pol, pol_t, KC, 4, 512, ev_pool)
    def ev_out(oc, ps, t):
        xt[oc] = dve.op(lambda e, i: e.scalar_tensor_tensor(out=x[:, oc, :], in0=ps, scalar=mod[:, 16 + oc:17 + oc],
                                                            in1=x[:, oc, :], op0=ALU.mult, op1=ALU.add), t, ada_t)
        return xt[oc]
    linear(g, mixed, mt, KC, KC, 256, ev_out)

    a = dve.op(lambda e, i: e.tensor_tensor(sc2[:, :], mod1[:, 32:40], g.p("g2"), ALU.mult), ada_t)
    ht = rms_norm(g, x, xt, sc2[:, :], mod[:, 24:32], h, sq, rs, scr, after=(a, pe.last))
    g.top = k_off
    route(g, h, ht)
    zero = g.area("zero", 512)
    assert g.top <= v_off
    zt = dve.op(lambda e, i: e.memset(zero[:, :], 0.0))
    for n in range(4):
        g.mm(g.bank[4 + n][:, :], zero[:, 0:P], zero[:, :], True, True, zt, g.banks.slots[4 + n].free, sig=True)
    gathered(g, h, ht, (g.base, k_off), (v_off, g.mod_off), a_tmp)
    g.only_if_over(lambda: experts(g, h, g.over, gate))
    toks = []
    for k in range(KC):
        ps = g.bank[4 + k // 2][:, (k % 2) * S:(k % 2 + 1) * S]
        toks.append(dve.op(lambda e, i, k=k, ps=ps: e.scalar_tensor_tensor(
            out=x[:, k, :], in0=ps, scalar=mod[:, 40 + k:41 + k], in1=x[:, k, :], op0=ALU.mult, op1=ALU.add)))
    for s in g.banks.slots[4:]:
        s.free = [toks[-1]]
    ht = rms_norm(g, x, toks, g.p("gf"), None, x, sq, rs, scr)
    return ht


def route(g, h, ht):
    dve, act = g.dve, g.act
    z = g.area("z", ST * 36)[:, :].rearrange("p (s f) -> p s f", s=ST)
    comb = g.area("comb", ST * NE)
    sel, one, tmp = (g.area(n, ST * NE) for n in ("rt_sel", "rt_one", "rt_tmp"))
    v4 = lambda a: a[:, :].rearrange("p (s n e) -> p s n e", s=ST, n=GROUPS)
    v3 = lambda a: a[:, :].rearrange("p (s e) -> p s e", s=ST)
    gr, goh = g.area("rt_g", ST * GROUPS), g.area("rt_goh", ST * GROUPS)
    g3, goh3 = (a[:, :].rearrange("p (s n) -> p s n", s=ST) for a in (gr, goh))
    ms = g.area("rt_m", 16 * ST)
    cnt = [0]

    def stat():
        cnt[0] += 1
        return ms[:, (cnt[0] - 1) * ST:cnt[0] * ST]

    def bc(a, n):
        return a.unsqueeze(2).to_broadcast([P, ST, n])

    t = None
    chain = [None]

    def d(fn, *needs):
        chain[0] = dve.op(fn, chain[0], *needs)
        return chain[0]

    for tt in range(ST):
        b = g.banks.take()
        for k in range(KC):
            t = g.mm(b.ap[:, 0:36], h[:, k, tt * P:(tt + 1) * P], g.p("w_router", k * 36, 36), k == 0, k == KC - 1,
                     ht[k], b.free, sig=(k == KC - 1))
        a = d(lambda e, i, b=b, tt=tt: e.tensor_tensor(z[:, tt, :], b.ap[:, 0:36], g.p("b_router"), ALU.add), t)
        b.free = [a]
    zg = z[:, :, 0:GROUPS]
    m, s, e1 = stat(), stat(), stat()
    first4 = g.c("first4").unsqueeze(1).to_broadcast([P, ST, GROUPS])
    first32 = g.c("first32").unsqueeze(1).to_broadcast([P, ST, NE])
    d(lambda e, i: e.tensor_reduce(m, zg, AX.X, ALU.max))
    d(lambda e, i: e.tensor_tensor(goh3, zg, bc(m, GROUPS), ALU.is_equal))
    d(lambda e, i: e.tensor_tensor(goh3, goh3, first4, ALU.mult))
    d(lambda e, i: e.tensor_reduce(e1, goh3, AX.X, ALU.max))
    d(lambda e, i: e.tensor_tensor(goh3, goh3, bc(e1, GROUPS), ALU.is_equal))
    a = d(lambda e, i: e.tensor_tensor(g3, zg, bc(m, GROUPS), ALU.subtract))
    a = act.op(lambda e, i: e.activation(gr[:, :], gr[:, :], ACT.Exp), a)
    pg = stat()
    d(lambda e, i: e.tensor_reduce(s, g3, AX.X, ALU.add), a)
    d(lambda e, i: e.reciprocal(pg, s))
    oh4 = goh3.unsqueeze(3).to_broadcast([P, ST, GROUPS, PER_GROUP])
    one4 = v4(one)
    for tt in range(ST):
        zt = z[:, tt, GROUPS:36].rearrange("p (n e) -> p n e", n=GROUPS)
        d(lambda e, i, tt=tt, zt=zt: e.tensor_tensor(v4(sel)[:, tt], zt, oh4[:, tt], ALU.mult))
        d(lambda e, i, tt=tt: e.tensor_scalar(one4[:, tt], oh4[:, tt], 1.0, -NEG, ALU.subtract, ALU.mult))
    d(lambda e, i: e.tensor_tensor(sel[:, :], sel[:, :], one[:, :], ALU.add))
    tops = []
    for n in range(2):
        mm_, fi = stat(), stat()
        oh = (one, tmp)[n]
        d(lambda e, i, mm_=mm_: e.tensor_reduce(mm_, v3(sel), AX.X, ALU.max))
        d(lambda e, i, mm_=mm_, oh=oh: e.tensor_tensor(v3(oh), v3(sel), bc(mm_, NE), ALU.is_equal))
        d(lambda e, i, oh=oh: e.tensor_tensor(v3(oh), v3(oh), first32, ALU.mult))
        d(lambda e, i, fi=fi, oh=oh: e.tensor_reduce(fi, v3(oh), AX.X, ALU.max))
        d(lambda e, i, fi=fi, oh=oh: e.tensor_tensor(v3(oh), v3(oh), bc(fi, NE), ALU.is_equal))
        if n == 0:
            d(lambda e, i, oh=oh: e.scalar_tensor_tensor(out=sel[:, :], in0=oh[:, :], scalar=3 * NEG, in1=sel[:, :],
                                                         op0=ALU.mult, op1=ALU.add))
        tops.append(mm_)
    df, w1, w2 = stat(), stat(), stat()
    a = d(lambda e, i: e.tensor_tensor(df, tops[1], tops[0], ALU.subtract))
    a = act.op(lambda e, i: e.activation(df, df, ACT.Exp), a)
    d(lambda e, i: e.tensor_scalar(w1, df, 1.0, None, ALU.add), a)
    d(lambda e, i: e.reciprocal(w1, w1))
    d(lambda e, i: e.tensor_tensor(w1, w1, pg, ALU.mult))
    d(lambda e, i: e.tensor_tensor(w2, w1, df, ALU.mult))
    ones_, twos_ = g.area("rt_1", ST * NE), g.area("rt_2", ST * NE)
    p_one, p_two = v3(ones_), v3(twos_)
    d(lambda e, i: e.tensor_copy(ones_[:, :], one[:, :]))
    d(lambda e, i: e.tensor_copy(twos_[:, :], tmp[:, :]))
    d(lambda e, i: e.tensor_tensor(v3(one), v3(one), bc(w1, NE), ALU.mult))
    d(lambda e, i: e.tensor_tensor(v3(tmp), v3(tmp), bc(w2, NE), ALU.mult))
    g.t_comb = d(lambda e, i: e.tensor_tensor(comb[:, :], one[:, :], tmp[:, :], ALU.add))
    W = NE + 2
    rank, sel_ = g.area("rank", ST * W), g.area("picked", ST * NE)
    comb2, over = g.area("comb2", ST * W), g.area("over", ST * NE)
    cnt_f = g.area("cnt_f", 1)
    g.rank, g.comb, g.over = (a[:, :].rearrange("p (s e) -> p s e", s=ST) for a in (rank, comb2, over))
    p3 = v3(sel_)
    g.slot_cst = g.area("slot_cst", P + 3 * SLOTS)
    tri, t_c = g.slot_cst[:, 0:P], Tok(g.s_slots, 16)
    d(lambda e, i: e.memset(comb2[:, :], 0.0))
    d(lambda e, i: e.memset(rank[:, :], -1.0))
    d(lambda e, i: e.tensor_copy(g.comb[:, :, 0:NE], v3(comb)))
    d(lambda e, i: e.tensor_tensor(v3(sel), p_one, p_two, ALU.max))
    a = d(lambda e, i: e.tensor_copy(sel_[:, :], sel[:, :]))
    b = g.banks.take()
    ps = b.ap
    g.mm(ps[:, 0:NE], tri, p3[:, 0, :], True, True, a, t_c, b.free)
    g.mm(ps[:, NE:2 * NE], g.c("ones"), p3[:, 0, :], True, False)
    g.mm(ps[:, NE:2 * NE], tri, p3[:, 1, :], False, True)
    g.mm(ps[:, 2 * NE:3 * NE], g.c("ones"), p3[:, 0, :], True, False)
    t = g.mm(ps[:, 2 * NE:3 * NE], g.c("ones"), p3[:, 1, :], False, True, sig=True)
    for tt in range(ST):
        d(lambda e, i, tt=tt: e.scalar_tensor_tensor(out=g.rank[:, tt, 0:NE], in0=ps[:, tt * NE:(tt + 1) * NE], scalar=1.0,
                                                     in1=p3[:, tt, :], op0=ALU.add, op1=ALU.mult), t)
    d(lambda e, i: e.tensor_scalar(g.rank[:, :, 0:NE], g.rank[:, :, 0:NE], 1.0, None, ALU.subtract))
    b.free = [d(lambda e, i: e.tensor_reduce(cnt_f[:, :], ps[:, 2 * NE:3 * NE], AX.X, ALU.max))]
    a = d(lambda e, i: e.tensor_copy(g.most[:, :], cnt_f[:, :]))
    dve.need(a)
    dve.raise_(g.s_flag)
    d(lambda e, i: e.tensor_scalar(g.over, g.rank[:, :, 0:NE], float(CAP), None, ALU.is_ge))
    g.t_rank = d(lambda e, i: e.tensor_tensor(g.over, g.over, v3(comb), ALU.mult))
    return comb


def turn_all(g, src, dst, group, *needs):
    banks = [g.bank[n][:, :] for n in range(4)]
    for n in range(4):
        for j, blk in enumerate(group(n)):
            t = g.mm(banks[n][:, j * P:(j + 1) * P], src(*blk), g.c("ident"), True, True, needs, g.banks.slots[n].free,
                     sig=(j == 3), transpose=True)
    toks = []
    for n in range(4):
        e = (g.act, g.dve)[n % 2]
        fn = (lambda e, i, n=n: e.copy(dst(n), banks[n])) if e is g.act else (lambda e, i, n=n: e.tensor_copy(dst(n), banks[n]))
        toks.append(e.op(fn, t))
        g.banks.slots[n].free = [toks[-1]]
    return toks


def gathered(g, h, ht, room0, room1, a_tmp):
    pe, act, dve, pool = g.pe, g.act, g.dve, g.pool
    HALF = TILE // 2
    NB = 2 * AHEAD
    NH = 2 * R
    off = room0[0]
    w_hi, w_lo = [], []
    for n in range(NB):
        t, off = g.at(f"w_hi{n}", off, HALF, F32R)
        w_hi.append(t)
    assert off <= room0[1]
    off = room1[0]
    for n in range(NB):
        t, off = g.at(f"w_lo{n}", off, HALF, F32R)
        w_lo.append(t)
    x_s, off = g.at("x_s", off, KC * 4 * SLOTS, F32R)
    a_s, off = g.at("a_s", off, EC * 4 * SLOTS, F32R)
    gy = [None, None]
    gy[0], off = g.at("gy0", off, 1024)
    gy[1], off = g.at("gy1", off, 1024)
    pick, off = g.at("pick", off, ST * P)
    pickw, off = g.at("pickw", off, ST * 2 * P)
    put, off = g.at("put", off, 2 * S)
    assert off <= room1[1]
    x_s = x_s[:, :].rearrange("p (k e h n) -> p k e h n", k=KC, e=2, h=2)
    a_s = a_s[:, :].rearrange("p (e f h n) -> p e f h n", e=2, f=EC, h=2)
    a_tmp = a_tmp[:, :].rearrange("p (e f n) -> p e f n", e=2, f=EC)
    h_tok = g.h[:, :].rearrange("p (s d) -> p s d", s=ST)
    iota2 = g.slot_cst[:, P:P + 2 * SLOTS]
    fold = g.slot_cst[:, P + 2 * SLOTS:P + 3 * SLOTS]

    turned = turn_all(g, lambda k, tt: h[:, k, tt * P:(tt + 1) * P], lambda n: h_tok[:, n // 2, (n % 2) * 512:(n % 2 + 1) * 512],
                      lambda n: [(4 * (n % 2) + j, n // 2) for j in range(4)], *ht)

    def picks(dst, width, first, weighted):
        t = None
        for tt in range(ST):
            for j in range(2):
                o = dst[:, (2 * tt + j) * width:(2 * tt + j + 1) * width]
                def fn(e, i, o=o, tt=tt, j=j):
                    ex = bass.ds(first(i) + j, 1)
                    w = g.comb[:, tt, ex] if weighted else None
                    return e.tensor_scalar(o, iota2[:, 0:width], g.rank[:, tt, ex], w, ALU.is_equal, *([ALU.mult] if weighted else []))
                t = dve.op(fn, g.t_rank if g.loop is None else None)
        return t

    banks = [g.bank[n][:, :] for n in range(4)]

    def gather(n, bank, *needs):
        for j in range(4):
            k = 4 * n + j
            for tt in range(ST):
                t = g.mm(banks[bank][:, j * P:(j + 1) * P], h_tok[:, tt, k * P:(k + 1) * P], pick[:, tt * P:(tt + 1) * P],
                         tt == 0, tt == 1, *needs, sig=(tt == 1 and j == 3))
        return t

    def cut_x(n, bank, *needs):
        src = banks[bank].rearrange("p (k e n) -> p k e n", k=4, e=2)
        hi, lo = x_s[:, 4 * n:4 * n + 4, :, 0, :], x_s[:, 4 * n:4 * n + 4, :, 1, :]
        a = act.op(lambda e, i: e.copy(hi, src), *needs)
        return a, dve.op(lambda e, i: e.tensor_tensor(lo, src, hi, ALU.subtract), a)

    tp = picks(pick, SLOTS, lambda i: 0, False)
    for n in range(2):
        t = gather(n, n, tp, *turned)
        cut_x(n, n, t)
    cut_hi, cut_lo, used = {}, {}, {}

    def cut(n, tiles, free):
        w, filled = tiles[n // 2]
        src = w[:, (n % 2) * HALF:(n % 2 + 1) * HALF]
        hi, lo = w_hi[n % NB][:, :], w_lo[n % NB][:, :]
        e = pool if n % 4 == 2 else dve
        cut_hi[n] = act.op(lambda e, i: e.copy(hi, src), filled, free)
        cut_lo[n] = e.op(lambda e, i: e.tensor_tensor(lo, src, hi, ALU.subtract), cut_hi[n], free, filled)

    first = [(g.ring[(g.tile + n) % R], Tok(g.s_slot[(g.tile + n) % R], 16 * ((g.tile + n) // R + 1))) for n in range(NB // 2)]
    for n in range(NB):
        cut(n, first, None)
    g.flush_tiles()
    g.meet(clear=False)
    g.open(0, NE // 2, counted=True)
    holds = {}

    def hold(e, key):
        lst = []
        holds.setdefault(key, []).append(lst)
        e.items.append(("hold", lst))

    tiles = [g.next_tile() for _ in range(R)]
    tiles += [(w, Tok(f.sem, f.n + 16, f.loop)) for w, f in tiles[:NB // 2]]

    def use(n, bank, stat, first, last, *needs):
        if n < NB:
            hold(pe, ("hi", n))
            hold(pe, ("lo", n))
        for j in range(2):
            for part, toks in ((w_hi, cut_hi), (w_lo, cut_lo)):
                t = g.mm(banks[bank], stat(j), part[n % NB][:, j * 512:(j + 1) * 512], first and j == 0 and part is w_hi,
                         last and j == 1 and part is w_lo, toks[n] if n >= NB else None, *needs, sig=(j == 1 and part is w_lo))
        used[n] = t
        if n % 2:
            g.done_tile()
        return t

    def up(ex, which):
        n0, bank = 8 * ex + 4 * which, 2 * ex + which
        hold(pe, ("bank", bank))
        for m in range(4):
            n = n0 + m
            t = use(n, bank, lambda j, m=m: x_s[:, 2 * m + j, ex].rearrange("p h n -> p (h n)"), m == 0, m == 3)
            if m == 3:
                dst = gy[ex][:, which * 512:(which + 1) * 512]
                if which == 0:
                    c = act.op(lambda e, i: e.copy(dst, banks[bank]), t)
                else:
                    c = dve.op(lambda e, i: e.tensor_copy(dst, banks[bank]), t)
            cut(n + NB, tiles, t)
        return t, c

    def fold_up(ex, bank, copied, *needs):
        for which in range(2):
            for f in range(EC):
                c = (which * EC + f) * SLOTS
                t = g.mm(banks[bank][:, c:c + SLOTS], gy[ex][:, which * 512 + f * P:which * 512 + (f + 1) * P], fold, True, True,
                         *copied, *needs, sig=(f == EC - 1))
        half = lambda which: banks[bank][:, which * 256:(which + 1) * 256].rearrange("p (f n) -> p f n", f=EC)
        tmp, hi, lo = a_tmp[:, ex], a_s[:, ex, :, 0, :], a_s[:, ex, :, 1, :]
        a = act.op(lambda e, i: e.activation(tmp, half(0), ACT.Silu), t)
        a = dve.op(lambda e, i: e.tensor_tensor(tmp, tmp, half(1), ALU.mult), a)
        read = a
        a = dve.op(lambda e, i: e.tensor_copy(hi, tmp), a)
        return read, [a, dve.op(lambda e, i: e.tensor_tensor(lo, tmp, hi, ALU.subtract), a)]

    def down(ex, half, bank, a_cut, *needs):
        for m in range(2):
            n = 16 + 4 * ex + 2 * half + m
            t = use(n, bank, lambda j, m=m: a_s[:, ex, 2 * m + j].rearrange("p h n -> p (h n)"), m == 0, m == 1, *a_cut, *needs)
            if m == 1:
                dst = gy[ex][:, half * 512:(half + 1) * 512]
                if half == 0:
                    c = act.op(lambda e, i: e.copy(dst, banks[bank]), t)
                else:
                    c = dve.op(lambda e, i: e.tensor_copy(dst, banks[bank]), t)
            cut(n + NB, tiles, t)
        return c

    def scatter(ex, t_put, y0, y1):
        for oc in range(KC):
            t = g.mm(g.bank[4 + oc // 2][:, (oc % 2) * S:(oc % 2 + 1) * S], gy[ex][:, oc * P:(oc + 1) * P],
                     put[:, ex * S:(ex + 1) * S], False, False, t_put, (y0, y1)[oc // 4], sig=(oc == KC - 1), skip=True)
        return t

    hold(pe, "x_hi")
    hold(pe, "x_lo")
    t, g0 = up(0, 0)
    hold(dve, "gather_read")
    t_p = picks(pick, SLOTS, lambda i: i * 2 + 2, False)
    t, u0 = up(0, 1)
    t, g1 = up(1, 0)
    read0, a0 = fold_up(0, 0, (g0, u0))
    tg0 = gather(0, 1, t_p, u0)
    t, u1 = up(1, 1)
    tg1 = gather(1, 2, t_p, g1)
    x0 = cut_x(0, 1, t)
    hold(dve, "put_read")
    t_w = picks(pickw, 2 * SLOTS, lambda i: i * 2, True)
    y00 = down(0, 0, 0, a0, read0)
    x1 = cut_x(1, 2, tg1)
    read1, a1 = fold_up(1, 3, (g1, u1))
    y01 = down(0, 1, 1, a0, *x0)
    for ex in range(2):
        for tt in range(ST):
            c = (ex * ST + tt) * P
            t = g.mm(banks[2][:, c:c + P], pickw[:, (2 * tt + ex) * P:(2 * tt + ex + 1) * P], g.c("ident"), True, True,
                     t_w, *x1, sig=(ex == 1 and tt == 1), transpose=True)
    put_read = t
    t_put = act.op(lambda e, i: e.copy(put[:, :], banks[2]), t)
    y10 = down(1, 0, 3, a1, read1)
    scatter(0, t_put, y00, y01)
    y11 = down(1, 1, 2, a1, t_put)
    scatter(1, t_put, y10, y11)
    ends = {"put_read": put_read, "gather_read": tg1, "x_hi": x1[0], "x_lo": x1[1],
            ("bank", 0): y00, ("bank", 1): y01, ("bank", 2): y11, ("bank", 3): y10}
    for n in range(NB):
        ends["hi", n], ends["lo", n] = cut_hi[NH + n], cut_lo[NH + n]
    for key, lists in holds.items():
        for lst in lists:
            lst.append(ends[key].before())
    g.fix_holds()
    assert g.to_free == 0
    g.close()
    g.meet(clear=False)


def experts(g, h, comb, work):
    pe, act, dve = g.pe, g.act, g.dve
    pe.raise_(g.s_over_freed)
    h_tok = g.h[:, :].rearrange("p (s d) -> p s d", s=ST)
    back = turn_all(g, lambda tt, k: h_tok[:, tt, k * P:(k + 1) * P],
                    lambda n: h[:, 2 * n:2 * n + 2, :].rearrange("p k t -> p (k t)"),
                    lambda n: [(tt, 2 * n + j) for j in range(2) for tt in range(ST)])
    pe.need(*back)
    act.need(*back)
    acts = [g.gate_area(work, n) for n in range(2)]
    diag = work[:, 3072:3072 + 2 * P]
    cbs = work[:, 3328:3328 + 2 * S]
    g.open(0, NE // 2, counted=True)
    banks = [g.bank[n][:, :] for n in range(4)]
    comb3 = comb
    last = {}

    bank_k = [0]
    bank_reader = {}
    first_wait = []

    def take():
        n = bank_k[0] % 4
        bank_k[0] += 1
        if n not in bank_reader:
            holder = []
            first_wait.append((n, holder))
            return n, holder
        return n, [bank_reader[n]]

    act_reader = {}
    for ex in range(2):
        A = acts[ex]
        n, free = take()
        cb_b = n
        if ex in (0, 1):
            hold_cb = []
            first_wait.append((("cb", ex), hold_cb))
        tds = []
        for tt in range(ST):
            tds.append(dve.op(lambda e, i, tt=tt, ex=ex: e.tensor_scalar(
                diag[:, tt * P:(tt + 1) * P], g.c("ident"), comb3[:, tt, bass.ds(i * 2 + ex, 1)], None, ALU.mult),
                *( [act_reader["diag"]] if "diag" in act_reader else [])))
        if "diag0" not in act_reader:
            act_reader["diag0"] = True
        pe.items.append(("hold", free))
        for tt in range(ST):
            t = g.mm(banks[n][:, tt * P:(tt + 1) * P], g.c("ones"), diag[:, tt * P:(tt + 1) * P], True, True, tds[tt], sig=True)
        act_reader["diag"] = t
        cb = cbs[:, ex * S:(ex + 1) * S]
        act.items.append(("hold", hold_cb))
        a_cb = act.op(lambda e, i, n=n, cb=cb: e.copy(cb, banks[n][:, 0:S]), t)
        bank_reader[n] = a_cb
        a_toks = []
        for half in range(2):
            for j in range(2):
                pair = []
                fc = 2 * half + j
                for which in range(2):
                    n, free = take()
                    pe.items.append(("hold", free))
                    for k in range(KC):
                        w, f = g.tile_at(4 * ex + 2 * which + k // 4)
                        c = (k % 4) * 512 + fc * P
                        t = g.mm(banks[n][:, 0:S], w[:, c:c + P], h[:, k, :], k == 0, k == KC - 1, f, sig=(k == KC - 1))
                    pair.append((n, t))
                (ng, tg), (nu, tu) = pair
                hold_a = []
                first_wait.append((("act", ex), hold_a))
                act.items.append(("hold", hold_a))
                a = act.op(lambda e, i, A=A, fc=fc, n=ng: e.activation(A[:, fc, :], banks[n][:, 0:S], ACT.Silu), tg)
                bank_reader[ng] = a
                a = dve.op(lambda e, i, A=A, fc=fc, n=nu: e.tensor_tensor(A[:, fc, :], A[:, fc, :], banks[n][:, 0:S], ALU.mult), a, tu)
                bank_reader[nu] = a
                a_toks.append(dve.op(lambda e, i, A=A, fc=fc, cb=cb: e.tensor_tensor(A[:, fc, :], A[:, fc, :], cb, ALU.mult), a, a_cb))
        for half in range(2):
            w, f = g.tile_at(8 + 2 * ex + half)
            for j in range(4):
                oc = 4 * half + j
                for k in range(EC):
                    t = g.mm(g.bank[4 + oc // 2][:, (oc % 2) * S:(oc % 2 + 1) * S],
                             w[:, k * 512 + j * P:k * 512 + (j + 1) * P], A[:, k, :], False, False, f, a_toks[k],
                             sig=(k == EC - 1 and j == 3), skip=True)
        last["act", ex] = t
        last["cb", ex] = a_toks[-1]
    pe.need(t)
    pe.raise_(g.s_over_freed)
    for key, holder in first_wait:
        if isinstance(key, int):
            holder.append(bank_reader[key].before())
        elif key[0] == "act":
            holder.append(last[key].before())
        else:
            holder.append(last[key].before())
    g.fix_holds()
    g.close()
    for n in range(AHEAD):
        pe.need(Tok(g.s_over[n], 16 * (NE // 2 + 1)))
    for e in g.engs:
        e.need(e.last)


def second_consts(g, rooms):
    act, dve = g.act, g.dve
    ang, kf, r, r2, lbs = rooms
    posi = g.posi
    ki = posi[:, :]
    two_pi = 2 * np.pi
    c1 = 6.28125
    c2 = 0.0019350051879882812
    c3 = two_pi - c1 - c2
    pi = float(np.nextafter(np.float32(np.pi), np.float32(0)))
    ch = [None]

    def d(fn, *needs):
        ch[0] = dve.op(fn, ch[0], *needs)
        return ch[0]

    d(lambda e, i: e.tensor_copy(ang, posi[:, :]), g.t_pos)
    d(lambda e, i: e.tensor_scalar(ang, ang, g.c("invf"), None, ALU.mult), g.t_cst)
    d(lambda e, i: e.tensor_scalar(kf, ang, 1.0 / two_pi, None, ALU.mult))
    d(lambda e, i: e.tensor_copy(ki, kf))
    d(lambda e, i: e.tensor_copy(kf, ki))
    d(lambda e, i: e.scalar_tensor_tensor(out=r, in0=kf, scalar=-c1, in1=ang, op0=ALU.mult, op1=ALU.add))
    d(lambda e, i: e.scalar_tensor_tensor(out=r, in0=kf, scalar=-c2, in1=r, op0=ALU.mult, op1=ALU.add))
    d(lambda e, i: e.scalar_tensor_tensor(out=r, in0=kf, scalar=-c3, in1=r, op0=ALU.mult, op1=ALU.add))
    d(lambda e, i: e.tensor_scalar(r2, r, np.pi / 2, None, ALU.add))
    d(lambda e, i: e.tensor_scalar(kf, r2, np.pi, -two_pi, ALU.is_gt, ALU.mult))
    d(lambda e, i: e.tensor_tensor(r2, r2, kf, ALU.add))
    for a in (r, r2):
        t = d(lambda e, i, a=a: e.tensor_scalar(a, a, pi, -pi, ALU.min, ALU.max))
    cos, sin = g.rope[:, 0:S], g.rope[:, S:2 * S]
    act.op(lambda e, i: e.activation(cos, r2, ACT.Sin), t)
    g.t_rope = act.op(lambda e, i: e.activation(sin, r, ACT.Sin), t)
    lb = g.lb
    raw = g.p("lb_raw")
    m, e0, s = lbs[:, 0:4], lbs[:, 4:12], lbs[:, 12:16]
    d(lambda e, i: e.tensor_tensor(m, raw[:, 0:4], raw[:, 4:8], ALU.max), g.t_prm)
    d(lambda e, i: e.tensor_tensor(e0[:, 0:4], raw[:, 0:4], m, ALU.subtract))
    t = d(lambda e, i: e.tensor_tensor(e0[:, 4:8], raw[:, 4:8], m, ALU.subtract))
    t = act.op(lambda e, i: e.activation(e0[:, :], e0[:, :], ACT.Exp), t)
    d(lambda e, i: e.tensor_tensor(s, e0[:, 0:4], e0[:, 4:8], ALU.add), t)
    d(lambda e, i: e.reciprocal(s, s))
    for l in range(2):
        d(lambda e, i, l=l: e.tensor_tensor(e0[:, 4 * l:4 * l + 4], e0[:, 4 * l:4 * l + 4], s, ALU.mult))
    d(lambda e, i: e.tensor_tensor(lb[:, 0:4], e0[:, 0:4], e0[:, 0:4], ALU.subtract))
    d(lambda e, i: e.tensor_tensor(m, e0[:, 0:4], e0[:, 4:8], ALU.add))
    d(lambda e, i: e.tensor_tensor(lb[:, 8:12], m, e0[:, 0:4], ALU.subtract))
    for l in range(2):
        t = d(lambda e, i, l=l: e.tensor_scalar(lb[:, 8 * l + 4:8 * l + 8], lb[:, 8 * l:8 * l + 4], -1.0, 1.0, ALU.mult, ALU.add))
    return t


def second_layer(g):
    pe, act, dve, pool = g.pe, g.act, g.dve, g.pool
    g.top = g.base
    x, h = (t[:, :].rearrange("p (k t) -> p k t", k=KC) for t in (g.x, g.h))
    chunked = lambda name, n: g.area(name, n * S)[:, :].rearrange("p (c t) -> p c t", c=n)
    sq = chunked("sq2", 8)
    rs, scr = g.area("rs2", S)[:, :], g.area("scr2", S)[:, :]
    q, sg, kk, cum = chunked("aq", 2), chunked("sg", 4), chunked("kk", 4), chunked("cum", 4)
    gsil = chunked("gs", 2)
    av, cv = (g.area(n, ST * w)[:, :].rearrange("p (s f) -> p s f", s=ST) for n, w in (("av", 256), ("cv", 512)))
    uT = chunked("uT", 2)
    cq, ck = chunked("cq", 4), chunked("ck", 4)
    mixed = chunked("mixed", 8)
    lead = g.c("ones", 0, 1).to_broadcast([P, S])
    cur = g.cur

    l0 = PRM["layer"][0]
    a = dve.op(lambda e, i: e.tensor_copy(cur[:, 0:16], g.prm[:, bass.ds(i * 16 + l0, 16)]))
    ct = dve.op(lambda e, i: e.tensor_copy(cur[:, 16:24], g.lb[:, bass.ds(i * 8, 8)]))
    ht = rms_norm(g, x, [None] * KC, cur[:, 0:8], None, h, sq, rs, scr, after=(a, ct))

    T = {}
    def ev(oc, ps, t):
        if oc < 2:
            a = act.op(lambda e, i: e.activation(q[:, oc, :], ps, ACT.Silu), t)
            T["q", oc] = a
        elif oc < 4:
            a = act.op(lambda e, i: e.activation(gsil[:, oc - 2, :], ps, ACT.Silu), t)
            T["g", oc - 2] = a
        elif oc < 8:
            n = oc - 4
            a = act.op(lambda e, i: e.activation(sg[:, n, :], ps, ACT.Sigmoid), t)
            f = dve.op(lambda e, i: e.tensor_scalar(sg[:, n, :], sg[:, n, :], cur[:, 20 + n:21 + n], cur[:, 16 + n:17 + n],
                                                    ALU.mult, ALU.add), a, ct)
            T["k", n] = dve.op(lambda e, i: e.tensor_scalar(kk[:, n, :], sg[:, n, :], -1.0, 1.0, ALU.mult, ALU.add), f)
            T["f", n] = dve.op(lambda e, i: e.tensor_scalar(sg[:, n, :], sg[:, n, :], 2.0 ** -64, None, ALU.max), T["k", n])
        elif oc < 10:
            a = act.op(lambda e, i: e.copy(uT[:, oc - 8, :], ps), t)
            T["u", oc - 8] = a
        else:
            n = oc - 10
            dst = (cq if n < 4 else ck)[:, n % 4, :]
            a = act.op(lambda e, i: e.copy(dst, ps), t)
            T["c", n] = a
        return a
    vt = []
    def ev_v(j, tt, ps, t):
        dst = av[:, tt, :] if j == 0 else cv[:, tt, (j - 1) * 256:j * 256]
        a = act.op(lambda e, i: e.copy(dst, ps), t)
        vt.append((j, a))
        return a

    def project(oc):
        linear(g, h, ht, 2, KC, 256, lambda n, ps, t: ev(oc + n, ps, t))

    def project_tokens(j):
        linear_tokens(g, h, ht, 256, lambda _, tt, ps, t: ev_v(j, tt, ps, t))

    project(4)
    project(6)
    a = act.op(lambda e, i: e.activation(sg, sg, ACT.Ln), *[T["f", n] for n in range(4)])
    for n in range(4):
        rev = slice(None, None, -1) if n >= 2 else slice(None)
        T["b", n] = dve.op(lambda e, i, n=n, rev=rev: e.tensor_tensor_scan(
            out=cum[:, n, rev], data0=lead, data1=sg[:, n, rev], initial=0.0, op0=ALU.mult, op1=ALU.add), a)

    mt = [None] * KC
    project(0)
    steps = hgrn(g, T, q, kk, cum, gsil, av, vt, mixed, mt, sq, sg)
    next(steps)
    project_tokens(0)
    project(2)
    project(8)
    project(10)
    next(steps)
    project(12)
    project(14)
    project(16)
    next(steps)
    project_tokens(1)
    next(steps)
    project_tokens(2)
    next(steps, None)
    cvt = [a for j, a in vt if j > 0]
    fourier(g, T, uT, cum, mixed, mt)

    rots = Rot([kk[:, 0:2, :], kk[:, 2:4, :]])
    cos, sin = (g.rope[:, o:o + S].unsqueeze(1).to_broadcast([P, 2, S]) for o in (0, S))
    qk_t = []
    for n in range(8):
        src = (cq if n < 4 else ck)
        if n % 2 == 0:
            b = g.banks.take()
        t = g.mm(b.ap[:, (n % 2) * S:(n % 2 + 1) * S], g.c("perm"), src[:, n % 4, :], True, True, T["c", n],
                 b.free if n % 2 == 0 else None, sig=True)
        if n % 2 == 1:
            c = n % 4
            s2 = src[:, c - 1:c + 1, :]
            rt = rots.take()
            r2 = rt.ap
            a = dve.op(lambda e, i, b=b, r2=r2: e.tensor_tensor(r2, b.ap[:, :].rearrange("p (c t) -> p c t", c=2), sin, ALU.mult), t, g.hgrn_read)
            b.free = [a]
            a2 = dve.op(lambda e, i, s2=s2: e.tensor_tensor(s2, s2, cos, ALU.mult), t)
            a = dve.op(lambda e, i, s2=s2, r2=r2: e.tensor_tensor(s2, s2, r2, ALU.add), a, a2)
            qk_t += [a, a]
    pbuf = Rot([g.m_all[:, i * S:(i + 1) * S] for i in range(8)])
    ptbuf = Rot([g.m_all[:, (8 + 2 * i) * S:(10 + 2 * i) * S] for i in range(4)])
    for b in pbuf.slots + ptbuf.slots:
        b.free = [g.hgrn_read]
    att = mixed[:, 4:8, :]
    g.small_used = 0
    at = []
    steps = attention(g, cq, ck, cv, [[qk_t[c], qk_t[4 + c]] for c in range(4)], cvt,
                   lambda hd, qt: g.c("lnmask", qt * S, S), None, False, att, pbuf, ptbuf, at)
    for _ in steps:
        pass
    mt[4:8] = at

    xt = [None] * KC
    def ev_out(oc, ps, t):
        xt[oc] = dve.op(lambda e, i: e.tensor_tensor(x[:, oc, :], x[:, oc, :], ps, ALU.add), t)
        return xt[oc]
    linear(g, mixed, mt, KC, KC, 256, ev_out)

    g.top = g.base
    g.top = g.base + 4 * (8 * S + 2 * S) + 256
    hid = g.area("hid", 32 * S)[:, :].rearrange("p (c t) -> p c t", c=32)
    over = (pe.last, dve.last, act.last, xt[-1])
    ht = rms_norm(g, x, xt, cur[:, 8:16], None, h, sq, rs, scr, after=(pe.last,))
    hd = []
    def ev_up(oc, ps, t):
        a = act.op(lambda e, i: e.activation(hid[:, oc, :], ps, ACT.Relu), t, *over)
        hd.append(dve.op(lambda e, i: e.tensor_tensor(hid[:, oc, :], hid[:, oc, :], hid[:, oc, :], ALU.mult), a))
        return a
    linear(g, h, ht, 32, KC, 256, ev_up)
    for oc in range(KC):
        b = g.banks.take()
        for half in range(2):
            w, f = g.next_tile()
            for k in range(16):
                fc = half * 16 + k
                t = g.mm(b.ap[:, 0:S], w[:, k * P:(k + 1) * P], hid[:, fc, :], fc == 0, fc == 31, f, hd[fc],
                         b.free if fc == 0 else None, sig=(fc == 31))
            g.done_tile()
        a = dve.op(lambda e, i, b=b, oc=oc: e.tensor_tensor(x[:, oc, :], x[:, oc, :], b.ap[:, 0:S], ALU.add), t)
        b.free = [a]
    g.flush_tiles()


def hgrn(g, T, q, kk, cum, gsil, av, vt, mixed, mt, sq, sg):
    pe, act, dve = g.pe, g.act, g.dve
    n_lv = len(LEVELS) + 1
    M = []
    ex = [mixed[:, 0:2, :], mixed[:, 2:4, :]]
    ex_free = [[], []]
    m_all = g.area("hm", n_lv * 2 * S)
    Mb = [m_all[:, n * 2 * S:(n + 1) * 2 * S].rearrange("p (c t) -> p c t", c=2) for n in range(n_lv)]
    g.m_all = m_all
    AT = sq[:, :, :].rearrange("p h t -> p (h t)").rearrange("p (h f) -> p h f", h=8)
    AL = g.area("hal", 8 * P)[:, :].rearrange("p (h f) -> p h f", h=8)
    tmp = mixed[:, 4:8, :].rearrange("p c t -> p (c t)")
    tmp_free = []
    at = {}
    m_free = []
    k_uses = 0
    for dr in range(2):
        M = []
        for lv, hh in enumerate((128,) + LEVELS):
            X, m = ex[k_uses % 2][:, 0:2, :], Mb[lv]
            xf = ex_free[k_uses % 2]
            nb = 2 * S // (2 * hh)
            split = lambda a, hh=hh: a.rearrange("p c (n s h) -> p (c n) s h", s=2, h=hh)
            cv = split(cum[:, 2 * dr:2 * dr + 2, :])
            mid = (cv[:, :, 0, hh - 1:hh] if dr == 0 else cv[:, :, 1, 0:1]).to_broadcast([P, nb, hh])
            subs = []
            for side in range(2):
                is_q = (side == 1) == (dr == 0)
                o, b_ = split(X)[:, :, side, :], cv[:, :, side, :]
                a0, a1 = (b_, mid) if is_q else (mid, b_)
                subs.append(dve.op(lambda e, i, o=o, a0=a0, a1=a1: e.tensor_tensor(o, a0, a1, ALU.subtract),
                                   T["b", 2 * dr], T["b", 2 * dr + 1], xf))
            a = act.op(lambda e, i, X=X: e.activation(X, X, ACT.Exp), *subs)
            for side in range(2):
                is_q = (side == 1) == (dr == 0)
                src = q if is_q else kk[:, 2 * dr:2 * dr + 2, :]
                o, xx, sv = split(m)[:, :, side, :], split(X)[:, :, side, :], split(src)[:, :, side, :]
                t = dve.op(lambda e, i, o=o, xx=xx, sv=sv: e.tensor_tensor(o, xx, sv, ALU.mult), a, m_free,
                           T["q", 0], T["q", 1], T["k", 2 * dr], T["k", 2 * dr + 1])
            ex_free[k_uses % 2] = [t]
            k_uses += 1
            M.append(t)
        yield
        for c in range(2):
            n = 2 * dr + c
            for tt in range(ST):
                for j in range(2):
                    hd, lo = 4 * dr + 2 * c + j, DH * j
                    b1, b2 = g.banks.take(), g.banks.take()
                    cols = slice(tt * P, (tt + 1) * P)
                    for lv in range(NL):
                        b = (b1, b2)[lv // 4]
                        if lv < NL - 1:
                            a_, b_ = Mb[lv + 1][lo:lo + DH, c, cols], Mb[lv + 1][lo:lo + DH, c, cols]
                        else:
                            a_, b_ = kk[lo:lo + DH, n, cols], q[lo:lo + DH, c, cols]
                        t = g.mm(b.ap[:, (lv % 4) * P:(lv % 4 + 1) * P], a_, b_, True, True, M, b.free, sig=(lv in (3, NL - 1)))
                        if lv == 3:
                            t1 = t
                    o = dr * NL * P
                    a1 = dve.op(lambda e, i, b=b1, o=o: e.tensor_tensor(tmp[:, 0:512], b.ap[:, :], g.c("hmask", o, 512), ALU.mult), t1, tmp_free)
                    a2 = dve.op(lambda e, i, b=b2, o=o: e.tensor_tensor(tmp[:, 512:1024], b.ap[:, :], g.c("hmask", o + 512, 512), ALU.mult), t)
                    b1.free, b2.free = [a1], [a2]
                    dst = AT[:, hd, tt * P:(tt + 1) * P]
                    a = dve.op(lambda e, i, dst=dst: e.tensor_reduce(dst, tmp.rearrange("p (l t) -> p t l", l=NL), AX.X, ALU.add), a1, a2)
                    tmp_free = [a]
                    at[hd, tt] = a
            for j in range(2):
                hd, lo = 4 * dr + 2 * c + j, DH * j
                b = g.banks.take()
                kt, qt = (0, 1) if dr == 0 else (1, 0)
                t = g.mm(b.ap[:, 0:P], Mb[0][lo:lo + DH, c, kt * P:(kt + 1) * P], Mb[0][lo:lo + DH, c, qt * P:(qt + 1) * P],
                         True, True, M, b.free, sig=True)
                a = act.op(lambda e, i, b=b, hd=hd: e.copy(AL[:, hd, :], b.ap[:, 0:P]), t)
                b.free = [a]
                at[hd, 2] = a
        m_free = [t]
    g.hgrn_read = [t, tmp_free, dve.last]
    avt = [a for j, a in vt if j == 0]
    o_, inv = sg[:, 0:2, :], sg[:, 2:4, :]
    tmp4 = mixed[:, 4:8, :]
    s2_, sc_ = tmp4[:, 0:2, :], tmp4[:, 2:4, :]
    sqt = []
    for c in range(2):
        b = g.banks.take()
        for j in range(2):
            lo = DH * j
            f, r = 2 * c + j, 4 + 2 * c + j
            vcol = slice((2 * c + j) * DH, (2 * c + j + 1) * DH)
            needs = [at[f, n] for n in range(3)] + [at[r, n] for n in range(3)] + avt + b.free
            q0, q1 = b.ap[lo:lo + DH, 0:P], b.ap[lo:lo + DH, P:S]
            g.mm(q0, av[:, 0, vcol], AT[:, f, 0:P], True, False, needs)
            g.mm(q0, av[:, 0, vcol], AT[:, r, 0:P], False, False)
            g.mm(q0, av[:, 1, vcol], AL[:, r, :], False, True)
            g.mm(q1, av[:, 0, vcol], AL[:, f, :], True, False)
            g.mm(q1, av[:, 1, vcol], AT[:, f, P:S], False, False)
            t = g.mm(q1, av[:, 1, vcol], AT[:, r, P:S], False, True, sig=True)
        a = act.op(lambda e, i, b=b, c=c: e.copy(o_[:, c, :], b.ap[:, 0:S]), t)
        b.free = [a]
        sqt.append(act.op(lambda e, i, c=c: e.activation(s2_[:, c, :], o_[:, c, :], ACT.Square), a, tmp_free))
    yield
    b = g.banks.take()
    for c in range(2):
        t = g.mm(b.ap[:, c * S:(c + 1) * S], g.c("headones"), s2_[:, c, :], True, True, sqt, b.free, sig=(c == 1))
    ps = b.ap[:, 0:2 * S].rearrange("p (c t) -> p c t", c=2)
    r, read = inv_rms(g, ps, inv, sc_, DH, t)
    b.free = [read]
    a = dve.op(lambda e, i: e.tensor_tensor(o_, o_, inv, ALU.mult), r, sqt)
    mt[0] = mt[1] = dve.op(lambda e, i: e.tensor_tensor(mixed[:, 0:2, :], o_, gsil, ALU.mult), a, T["g", 0], T["g", 1])
    yield


def fourier(g, T, uT, V, mixed, mt):
    act, dve = g.act, g.dve
    V = V[:, :, :].rearrange("p a t -> p (a t)").rearrange("p (s c f) -> p s c f", s=ST, c=2)
    vt = []
    for c in range(2):
        for tt in range(ST):
            b = g.banks.take()
            t = g.mm(b.ap[:, 0:S], uT[:, c, tt * P:(tt + 1) * P], g.c("dft_c"), True, True, T["u", c], b.free, sig=True)
            a = act.op(lambda e, i, b=b, c=c, tt=tt: e.copy(V[:, tt, c, :], b.ap[:, 0:S]), t, g.hgrn_read)
            b.free = [a]
            vt.append(a)
    for c in range(2):
        b = g.banks.take()
        for n in range(4):
            part, tt = n // 2, n % 2
            t = g.mm(b.ap[:, 0:S], V[:, tt, c, part * P:(part + 1) * P], g.c("dft_t", (part * ST + tt) * S, S), n == 0, n == 3,
                     vt, b.free, sig=(n == 3))
        a = act.op(lambda e, i, b=b, c=c: e.copy(mixed[:, 2 + c, :], b.ap[:, 0:S]), t, g.hgrn_read)
        b.free = [a]
        mt[2 + c] = a


def build(nc, ctx, dram, out):
    g = Prog(nc, ctx, dram, out)
    g.lb = ctx.enter_context(nc.sbuf_tensor("lb", [P, 16], F32))
    g.posi = ctx.enter_context(nc.sbuf_tensor("posi", [P, S], I32))
    g.most = ctx.enter_context(nc.sbuf_tensor("most", [P, 1], I32))
    g.base = (nc.sbuf_base + 31) // 32 * 32
    g.gate_area = lambda work, n: work[:, n * 1024:(n + 1) * 1024].rearrange("p (c t) -> p c t", c=EC)

    def fix_holds():
        for e in g.engs:
            new = []
            for it in e.items:
                if it[0] == "hold":
                    new += [("wait", t) for t in it[1]]
                else:
                    new.append(it)
            e.items[:] = new
    g.fix_holds = fix_holds
    g.t_prm, g.t_cst, g.t_tab = Tok(g.s_prm, 16), Tok(g.s_cst, 16), Tok(g.s_tab, 48)
    g.t_pool_a, g.t_pos = Tok(g.s_cst, 16), Tok(g.s_pos, 16)
    g.t_pool_a = Tok(g.s_pos, 32)
    g.t_pos = g.t_pool_a
    tx = Tok(g.s_x, 16)

    for e in g.engs:
        e.need(tx, g.t_prm, g.t_cst)
    xt = first_block(g, [tx] * KC)
    g.dve.need(Tok(g.s_mask, 16))
    g.meet(clear=True)
    g.open(0, DEPTH2, counted=False)
    second_layer(g)
    g.meet(clear=True)
    g.close()
    x, h = (t[:, :].rearrange("p (k t) -> p k t", k=KC) for t in (g.x, g.h))
    g.top = g.base
    sq = g.area("sqf", KC * S)[:, :].rearrange("p (c t) -> p c t", c=KC)
    rs, scr = g.area("rsf", S)[:, :], g.area("scrf", S)[:, :]
    final = rms_norm(g, x, [None] * KC, g.p("gf2"), None, h, sq, rs, scr)
    assert g.tile == N_TILES, (g.tile, N_TILES)

    a0, a1 = CST["pool_a"]
    assert a1 - a0 == 2 * NL * P
    with nc.Block() as block:
        @block.sync
        def _(sp):
            sp.dma_start(g.x[:, :], dram["x"]).then_inc(g.s_x, 16)
            sp.dma_start(g.prm[:, :], dram["prm"]).then_inc(g.s_prm, 16)
            for s in range(R):
                sp.dma_start(g.ring[s][:, :], dram["weights"][s]).then_inc(g.s_slot[s], 16)
            tile = lambda t: dram["weights"][bass.ds(t, 1)].rearrange("a p f -> (a p) f")

            def stream(lo, hi):
                with sp.Fori(lo, hi) as i:
                    for s in range(R):
                        sp.wait_ge(g.s_freed, (i - 1) * R + s + 1)
                        sp.dma_start(g.ring[s][:, :], tile(i * R + s)).then_inc(g.s_slot[s], 16)

            stream(1, R_LAYERS)
            for s in range(AHEAD):
                sp.wait_ge(g.s_freed, (R_LAYERS - 1) * R + s + 1)
                sp.dma_start(g.ring[s][:, :], dram["weights"][R_LAYERS * R + s]).then_inc(g.s_slot[s], 16)
            sp.wait_ge(g.s_flag, 1)
            most = sp.value_load(g.most[0:1, 0:1])
            with sp.If(most > CAP):
                sp.wait_ge(g.s_over_freed, 1)
                for s in range(R):
                    sp.dma_start(g.ring[s][:, :], dram["weights"][R_EXPERTS * R + s]).then_inc(g.s_over[s], 16)
                with sp.Fori(1, NE // 2) as i:
                    sp.wait_ge(g.s_over_freed, i + 1)
                    for s in range(R):
                        sp.dma_start(g.ring[s][:, :], tile((i + R_EXPERTS) * R + s)).then_inc(g.s_over[s], 16)
                sp.wait_ge(g.s_over_freed, NE // 2 + 1)
                for s in range(AHEAD):
                    sp.dma_start(g.ring[s][:, :], dram["weights"][R_LAYERS * R + s]).then_inc(g.s_over[s], 16)
            for s in range(AHEAD, R):
                sp.wait_ge(g.s_freed, (R_LAYERS - 1) * R + s + 1)
                sp.dma_start(g.ring[s][:, :], dram["weights"][R_LAYERS * R + s]).then_inc(g.s_slot[s], 16)
            stream(R_LAYERS + 1, N_TILES // R)

        @block.scalar
        def _(e):
            e.dma_start(g.cst[:, :], dram["cst"][:, 0:a0]).then_inc(g.s_cst, 16)
            e.dma_start(g.tab[0:BUCKETS, :], dram["tab"][0:BUCKETS, :]).then_inc(g.s_tab, 16)
            e.dma_start(g.tab_neg[0:HEADS, :], dram["tab"][BUCKETS:BUCKETS + 1, :].to_broadcast([HEADS, NB_ROW])).then_inc(g.s_tab, 16)
            e.dma_start(g.rb[0:BUCKETS, :], dram["rel"]).then_inc(g.s_tab, 16)
            e.dma_start(g.pool_a[:, :], dram["cst"][:, a0:a1]).then_inc(g.s_pos, 16)
            e.dma_start(g.posi[:, :], dram["pos"].to_broadcast([P, S])).then_inc(g.s_pos, 16)
            g.act.emit(e)
            for n in range(2):
                t = final[4 * n + 3]
                e.wait_ge(t.sem, t.n)
                cols = slice(n * 4 * S, (n + 1) * 4 * S)
                e.dma_start(out[:, cols], g.h[:, cols]).then_inc(g.s_out, 16)
            e.wait_ge(g.s_out, 32)

        @block.tensor
        def _(e):
            g.pe.emit(e)

        @block.vector
        def _(e):
            g.dve.emit(e)

        @block.gpsimd
        def _(e):
            e.wait_ge(g.t_row.sem, g.t_row.n)
            e.dma_start(dram["row"], g.row[0:HEADS, :]).then_inc(g.s_row, 16)
            e.wait_ge(g.s_row, 16)
            for qt in range(ST):
                nk = (qt + 1) * P
                src = bass.AP(dram["row"].tensor, 0, [[1, P], [NB_ROW, HEADS], [1, nk]])
                o = 0 if qt == 0 else HEADS * P
                e.dma_start(g.bias[:, o:o + HEADS * nk].rearrange("p (h k) -> p h k", h=HEADS), src).then_inc(g.s_bias, 16)
            e.wait_ge(g.s_bias, 32)
            e.wait_ge(g.t_pooled.sem, g.t_pooled.n)
            e.dma_start(g.pool_a[:, :], dram["cst"][:, a1:]).then_inc(g.s_mask, 16)
            e.wait_ge(g.t_k_free.sem, g.t_k_free.n)
            e.dma_start(g.slot_cst[:, :], dram["slots"]).then_inc(g.s_slots, 16)
            g.pool.emit(e)


def kernel(**inputs):
    from contextlib import ExitStack
    import concourse.bacc as bacc
    from concourse.bass_utils import run_bass_kernel_spmd

    a = {k: np.asarray(v) for k, v in inputs.items()}
    vec = lambda v: v.reshape(-1, P).T

    def cols(w, width):
        k, n = w.shape
        return w.reshape(k // P, P, n // width, width).transpose(2, 1, 0, 3).reshape(-1, P, (k // P) * width)

    w_in = a["w_in"][0]
    turns = np.stack([cols(a["w_ada"][0][:, 2048:], 256), cols(w_in, 256)], 1).reshape(-1, P, TILE)
    tiles = [cols(a["w_ada"][0][:, :2048], 256), turns,
             cols(a["w_branch_attn"][0], 512), cols(a["w_branch_pool"][0], 512), cols(a["w_out"][0], 256)]
    n0 = sum(t.shape[0] for t in tiles)
    wg, wu = (a[n][0].reshape(NE, 2, 4, P, DE).transpose(0, 1, 3, 2, 4).reshape(NE, 2, P, TILE)
              for n in ("w_expert_gate", "w_expert_up"))
    wd = a["w_expert_down"][0].reshape(NE, EC, P, 2, 512).transpose(0, 3, 2, 1, 4).reshape(NE, 2, P, TILE)
    up = np.concatenate([wg, wu], 1).reshape(NE // 2, 8, P, TILE)
    ex = np.concatenate([up, wd.reshape(NE // 2, 4, P, TILE)], 1).reshape(-1, P, TILE)
    tiles.append(ex)
    for l in range(DEPTH2):
        w = a["w_in_2"][l]
        W = 256
        part = lambda lo, n: w[:, lo:lo + n]
        order = [part(2 * W, W), part(3 * W, W), part(0, W), part(W, W), part(4 * W, W), part(5 * W, W),
                 part(6 * W, 1536)]
        tiles += [cols(o, 256) for o in order]
        tiles += [cols(a["w_out_2"][l], 256), cols(a["w_up_2"][l], 256)]
        wdn = a["w_down_2"][l].reshape(2, 16, P, KC, P).transpose(3, 0, 2, 1, 4).reshape(-1, P, TILE)
        tiles.append(wdn)
    weights = np.concatenate([t.reshape(-1, P, TILE) for t in tiles])
    assert weights.shape[0] == N_TILES, weights.shape

    prm = np.zeros((P, N_PRM), np.float32)

    def put(name, v):
        lo, hi = PRM[name]
        prm[:, lo:hi] = v.reshape(P, hi - lo)

    put("b_ada", vec(a["b_ada"][0]))
    put("g1", vec(a["norm1_g"][0]))
    put("b_gate", vec(a["b_gate"][0]))
    put("pool_scale", vec(a["pool_scale"][0]))
    put("g2", vec(a["norm2_g"][0]))
    put("gf", vec(a["norm_f_g"]))
    put("c", vec(a["c"][0]))
    put("gf2", vec(a["final_norm_w_2"]))
    put("layer", np.concatenate([v for l in range(DEPTH2) for v in (vec(a["attn_norm_w_2"][l]), vec(a["mlp_norm_w_2"][l]))], 1))
    put("lb_raw", vec(a["hgrn_lower_bounds_2"].reshape(-1)))
    put("b_router", np.broadcast_to(np.concatenate([a["b_router_group"][0], a["b_router_expert"][0]]), (P, 36)))
    wr = np.concatenate([a["w_router_group"][0], a["w_router_expert"][0]], 1)
    put("w_router", wr.reshape(KC, P, 36).transpose(1, 0, 2))
    put("pool_w", a["pool_w"][0].transpose(1, 0, 2))
    x = np.ascontiguousarray(a["x"][0].T.reshape(KC, P, S).transpose(1, 0, 2)).reshape(P, KC * S)
    arrays = {"weights": weights, "prm": prm, "x": x, "cst": constants(), "tab": bias_table(), "slots": slot_constants(),
              "rel": np.ascontiguousarray(a["rel_bias"]), "pos": np.ascontiguousarray(a["positions_2"]).astype(np.int32).reshape(1, S)}

    nc = bacc.Bacc("TRN2", target_bir_lowering=False, num_devices=1)
    dram = {k: nc.dram_tensor("in_" + k, v.shape, mybir.dt.from_np(v.dtype), kind="ExternalInput").ap() for k, v in arrays.items()}
    dram["row"] = nc.dram_tensor("bias_rows", (HEADS, NB_ROW), F32, kind="Internal").ap()
    out = nc.dram_tensor("out", (P, KC * S), F32, kind="ExternalOutput").ap()
    with ExitStack() as ctx:
        build(nc, ctx, dram, out)
    r = run_bass_kernel_spmd(nc, [{"in_" + k: v for k, v in arrays.items()}], core_ids=[0])
    y = r.results[0]["out"].reshape(P, KC, S)
    return y.transpose(2, 1, 0).reshape(1, S, D)
```
